# Optimizing a Trainium2 kernel written in Bass

```python
import math
import jax, jax.numpy as jnp
from jax import lax
import numpy as np

D_MODEL = 2048
BATCH = 1
SEQ = 512
DEPTH = 1
DEC_BATCH = 8
DEC_SEQ = 1
PAST_LEN = 512
PAGE_SIZE = 128

A_HEADS = 8
A_DIM = 64
A_WIDTH = A_HEADS * 2 * A_DIM
S_HEADS = 16
S_HEAD_DIM = 64
S_INNER = S_HEADS * S_HEAD_DIM
S_GROUPS = 2
S_STATE = 128
S_CONV = 4
S_CHUNK = 128
S_CONV_DIM = S_INNER + 2 * S_GROUPS * S_STATE
MIX_WIDTH = A_WIDTH + S_INNER
SPLITS = (A_WIDTH, 2 * A_WIDTH, 3 * A_WIDTH, 3 * A_WIDTH + S_INNER, 3 * A_WIDTH + S_INNER + S_CONV_DIM)
IN_COLS = 3 * A_WIDTH + S_INNER + S_CONV_DIM + S_HEADS
N_MEM = 256
X_HEADS = 4
X_DIM = 128
X_WIDTH = X_HEADS * X_DIM
P_HEADS = 8
P_NKEYS = 128
P_EXPERTS = P_NKEYS * P_NKEYS
P_DKEY = 128
P_TOPK = 16
P_BLOCK = 128
Q_BLOCK = 128
EPS = 1e-6
F32 = jnp.float32

kernel_name = 'hymba_diffattn_ssd_peer_decode_step'

def rmsnorm(x, g):
    xf = x.astype(F32)
    y = xf * lax.rsqrt(jnp.mean(xf * xf, axis=-1, keepdims=True) + EPS)
    return (y * g.astype(F32)).astype(x.dtype)

def lambda_init(layer_idx):
    return 0.8 - 0.6 * math.exp(-0.3 * layer_idx)

def diff_weights(s, lam):
    p = jax.nn.softmax(s, axis=-1)
    return p[:, :, 0] - lam * p[:, :, 1]

def causal_conv(u, prev, w, bias):
    L = u.shape[1]
    up = jnp.concatenate([prev.astype(u.dtype), u], axis=1)
    out = bias
    for j in range(S_CONV):
        out = out + w[j] * up[:, j:j + L]
    return out, up[:, L:]

def segsum(a):
    T = a.shape[-1]
    ar = jnp.broadcast_to(a[..., :, None], a.shape + (T,))
    ar = jnp.where(jnp.tril(jnp.ones((T, T), bool), -1), ar, 0.0)
    ss = jnp.cumsum(ar, axis=-2)
    return jnp.where(jnp.tril(jnp.ones((T, T), bool)), ss, -jnp.inf)

def ssd_scan(x, dt, A, B, C, h0):
    b, L, H, P = x.shape
    n_chunks = -(-L // S_CHUNK)
    pad = n_chunks * S_CHUNK - L
    padf = lambda t: jnp.pad(t, [(0, 0), (0, pad)] + [(0, 0)] * (t.ndim - 2))
    x, dt, B, C = padf(x), padf(dt), padf(B), padf(C)
    ch = lambda t: t.reshape((b, n_chunks, S_CHUNK) + t.shape[2:])
    X = ch(x * dt[..., None].astype(x.dtype))
    Bc, Cc = ch(B), ch(C)
    a = jnp.moveaxis(ch(dt * A), -1, 1)
    a_cum = jnp.cumsum(a, axis=-1)
    Lmat = jnp.exp(segsum(a))
    y_diag = jnp.einsum('bclhn,bcshn,bhcls,bcshp->bclhp', Cc, Bc, Lmat, X)
    decay_states = jnp.exp(a_cum[..., -1:] - a_cum)
    states = jnp.einsum('bclhn,bhcl,bclhp->bchpn', Bc, decay_states, X)
    states = jnp.concatenate([h0[:, None].astype(states.dtype), states], axis=1)
    chunk_decay = jnp.exp(segsum(jnp.pad(a_cum[..., -1], [(0, 0), (0, 0), (1, 0)])))
    states = jnp.einsum('bhzc,bchpn->bzhpn', chunk_decay, states)
    y_off = jnp.einsum('bclhn,bchpn,bhcl->bclhp', Cc, states[:, :-1], jnp.exp(a_cum))
    y = (y_diag + y_off).reshape(b, n_chunks * S_CHUNK, H, P)[:, :L]
    return y, states[:, -1]

def memory_kv(mem, lw):
    b, m_len, _ = mem.shape
    m = rmsnorm(mem, lw['norm_mem'])
    mk = rmsnorm((m @ lw['wk_x']).reshape(b, m_len, X_HEADS, X_DIM), lw['kx_norm'])
    mv = (m @ lw['wv_x']).reshape(b, m_len, X_HEADS, X_DIM)
    return mk, mv

def peer(t, wq, keys, u_tab, v_tab):
    T = t.shape[0]
    nb = -(-T // P_BLOCK)
    tp = jnp.pad(t, [(0, nb * P_BLOCK - T), (0, 0)]).reshape(nb, P_BLOCK, D_MODEL)

    def block(tb):
        q = (tb @ wq).reshape(P_BLOCK, P_HEADS, 2, P_DKEY // 2)
        s = jnp.einsum('thcd,chkd->thck', q, keys.astype(q.dtype)).astype(F32)
        sv, si = lax.top_k(s, P_TOPK)
        cand = sv[..., 0, :, None] + sv[..., 1, None, :]
        cid = si[..., 0, :, None] * P_NKEYS + si[..., 1, None, :]
        fs, fi = lax.top_k(cand.reshape(P_BLOCK, P_HEADS, P_TOPK * P_TOPK), P_TOPK)
        eid = jnp.take_along_axis(cid.reshape(P_BLOCK, P_HEADS, P_TOPK * P_TOPK), fi, axis=-1)
        g = jax.nn.softmax(fs, axis=-1)
        act = jax.nn.gelu(jnp.einsum('td,thkd->thk', tb, u_tab[eid]).astype(F32), approximate=False)
        w = (g * act).astype(tb.dtype)
        return jnp.einsum('thk,thkd->td', w, v_tab[eid])

    return lax.map(block, tp).reshape(nb * P_BLOCK, D_MODEL)[:T]

def decoder_layer(x, layer_idx, lw, mem_k, mem_v, conv_prev, ssm_prev, past_k, past_v):
    b, L, _ = x.shape
    h = rmsnorm(x, lw['norm_mix'])
    proj = h @ lw['w_in']
    q, k, v, z, xbc, dt = jnp.split(proj, SPLITS, axis=-1)
    q = rmsnorm(q.reshape(b, L, A_HEADS, 2, A_DIM), lw['q_norm'])
    k = rmsnorm(k.reshape(b, L, A_HEADS, 2, A_DIM), lw['k_norm'])
    v = v.reshape(b, L, A_HEADS, 2 * A_DIM)
    lam0 = lambda_init(layer_idx)
    lam = (jnp.exp(jnp.sum(lw['lambda_q1'].astype(F32) * lw['lambda_k1'].astype(F32)))
           - jnp.exp(jnp.sum(lw['lambda_q2'].astype(F32) * lw['lambda_k2'].astype(F32))) + lam0)
    scale = A_DIM ** -0.5
    if past_k is None:
        nb = L // Q_BLOCK
        qb = jnp.moveaxis(q.reshape(b, nb, Q_BLOCK, A_HEADS, 2, A_DIM), 1, 0)
        k_pos = jnp.arange(L)

        def attend_block(args):
            qi, start = args
            s = jnp.einsum('bqhmd,bkhmd->bhmqk', qi, k).astype(F32) * scale
            q_pos = start + jnp.arange(Q_BLOCK)
            s = jnp.where(k_pos[None, :] <= q_pos[:, None], s, -jnp.inf)
            a = diff_weights(s, lam).astype(v.dtype)
            return jnp.einsum('bhqk,bkhe->bqhe', a, v)

        o = lax.map(attend_block, (qb, jnp.arange(nb) * Q_BLOCK))
        o = jnp.moveaxis(o, 0, 1).reshape(b, L, A_HEADS, 2 * A_DIM)
    else:
        P = past_k.shape[1]
        kp = past_k.reshape(b, P, A_HEADS, 2, A_DIM).astype(q.dtype)
        s_past = jnp.einsum('bqhmd,bkhmd->bhmqk', q, kp).astype(F32) * scale
        s_new = jnp.einsum('bqhmd,bkhmd->bhmqk', q, k).astype(F32) * scale
        s_new = jnp.where(jnp.tril(jnp.ones((L, L), bool)), s_new, -jnp.inf)
        a = diff_weights(jnp.concatenate([s_past, s_new], axis=-1), lam).astype(v.dtype)
        o = (jnp.einsum('bhqk,bkhe->bqhe', a[..., :P], past_v.astype(v.dtype))
             + jnp.einsum('bhqk,bkhe->bqhe', a[..., P:], v))
    o = rmsnorm(o, lw['subln']) * (1.0 - lam0)
    xbc, conv_state = causal_conv(xbc, conv_prev, lw['conv_w'], lw['conv_b'])
    xbc = jax.nn.silu(xbc)
    xs, Bm, Cm = jnp.split(xbc, (S_INNER, S_INNER + S_GROUPS * S_STATE), axis=-1)
    xs = xs.reshape(b, L, S_HEADS, S_HEAD_DIM)
    rep = S_HEADS // S_GROUPS
    Bm = jnp.repeat(Bm.reshape(b, L, S_GROUPS, S_STATE), rep, axis=2)
    Cm = jnp.repeat(Cm.reshape(b, L, S_GROUPS, S_STATE), rep, axis=2)
    dtv = jax.nn.softplus(dt.astype(F32) + lw['dt_bias'].astype(F32))
    A = -jnp.exp(lw['a_log'].astype(F32))
    y, ssm_state = ssd_scan(xs, dtv, A, Bm, Cm, ssm_prev)
    y = y + lw['d_skip'][:, None] * xs
    y = rmsnorm(y.reshape(b, L, S_INNER) * jax.nn.silu(z), lw['ssm_norm'])
    mixed = jnp.concatenate([o.reshape(b, L, A_WIDTH), y.astype(o.dtype)], axis=-1)
    x = x + mixed @ lw['w_out']
    hx = rmsnorm(x, lw['norm_x'])
    qx = rmsnorm((hx @ lw['wq_x']).reshape(b, L, X_HEADS, X_DIM), lw['qx_norm'])
    sx = jnp.einsum('bqhd,bmhd->bhqm', qx, mem_k.astype(qx.dtype)).astype(F32) * (X_DIM ** -0.5)
    px = jax.nn.softmax(sx, axis=-1).astype(mem_v.dtype)
    ox = jnp.einsum('bhqm,bmhd->bqhd', px, mem_v).reshape(b, L, X_WIDTH)
    x = x + ox.astype(x.dtype) @ lw['wo_x']
    hf = rmsnorm(x, lw['norm_ffn'])
    x = x + peer(hf.reshape(b * L, D_MODEL), lw['peer_wq'], lw['peer_keys'], lw['peer_u'], lw['peer_v']).reshape(b, L, D_MODEL)
    k_rows = k.reshape(b, L, A_HEADS, 2 * A_DIM)
    return x, k_rows, v, conv_state, ssm_state

def setup_inputs(seed: int = 0) -> dict:
    key = jax.random.key(seed)
    ks = iter(jax.random.split(key, 48))
    nrm = lambda shape, scale=1.0: jax.random.normal(next(ks), shape, F32) * scale
    gain = lambda shape: 1.0 + 0.02 * jax.random.normal(next(ks), shape, F32)
    n_pages = PAST_LEN // PAGE_SIZE
    n_used = DEC_BATCH * n_pages
    n_pool = n_used + max(1, n_used // 4)
    inp = {}
    inp['x_prompt'] = nrm((BATCH, SEQ, D_MODEL))
    inp['x_sample'] = nrm((DEC_BATCH, DEC_SEQ, D_MODEL))
    inp['cache_k'] = nrm((DEPTH, n_pool, PAGE_SIZE, A_HEADS, 2 * A_DIM))
    inp['cache_v'] = nrm((DEPTH, n_pool, PAGE_SIZE, A_HEADS, 2 * A_DIM))
    inp['cache_mem_k'] = nrm((DEPTH, DEC_BATCH, N_MEM, X_HEADS, X_DIM))
    inp['cache_mem_v'] = nrm((DEPTH, DEC_BATCH, N_MEM, X_HEADS, X_DIM))
    inp['state_conv'] = nrm((DEPTH, DEC_BATCH, S_CONV - 1, S_CONV_DIM))
    inp['state_ssm'] = nrm((DEPTH, DEC_BATCH, S_HEADS, S_HEAD_DIM, S_STATE), 0.1)
    inp['page_table'] = jax.random.permutation(next(ks), n_pool)[:n_used].reshape(DEC_BATCH, n_pages).astype(jnp.int32)
    inp['mem_prompt'] = nrm((BATCH, N_MEM, D_MODEL))
    inp['norm_mix'] = gain((DEPTH, D_MODEL))
    inp['w_in'] = nrm((DEPTH, D_MODEL, IN_COLS), D_MODEL ** -0.5)
    inp['q_norm'] = gain((DEPTH, A_DIM))
    inp['k_norm'] = gain((DEPTH, A_DIM))
    inp['lambda_q1'] = nrm((DEPTH, A_DIM), 0.1)
    inp['lambda_k1'] = nrm((DEPTH, A_DIM), 0.1)
    inp['lambda_q2'] = nrm((DEPTH, A_DIM), 0.1)
    inp['lambda_k2'] = nrm((DEPTH, A_DIM), 0.1)
    inp['subln'] = gain((DEPTH, 2 * A_DIM))
    inp['conv_w'] = nrm((DEPTH, S_CONV, S_CONV_DIM), S_CONV ** -0.5)
    inp['conv_b'] = nrm((DEPTH, S_CONV_DIM), 0.02)
    dt0 = jnp.exp(jax.random.uniform(next(ks), (DEPTH, S_HEADS), F32, math.log(1e-3), math.log(1e-1)))
    inp['dt_bias'] = dt0 + jnp.log(-jnp.expm1(-dt0))
    inp['a_log'] = jnp.log(jax.random.uniform(next(ks), (DEPTH, S_HEADS), F32, 1.0, 16.0))
    inp['d_skip'] = gain((DEPTH, S_HEADS))
    inp['ssm_norm'] = gain((DEPTH, S_INNER))
    inp['w_out'] = nrm((DEPTH, MIX_WIDTH, D_MODEL), MIX_WIDTH ** -0.5)
    inp['norm_x'] = gain((DEPTH, D_MODEL))
    inp['norm_mem'] = gain((DEPTH, D_MODEL))
    inp['wq_x'] = nrm((DEPTH, D_MODEL, X_WIDTH), D_MODEL ** -0.5)
    inp['wk_x'] = nrm((DEPTH, D_MODEL, X_WIDTH), D_MODEL ** -0.5)
    inp['wv_x'] = nrm((DEPTH, D_MODEL, X_WIDTH), D_MODEL ** -0.5)
    inp['qx_norm'] = gain((DEPTH, X_DIM))
    inp['kx_norm'] = gain((DEPTH, X_DIM))
    inp['wo_x'] = nrm((DEPTH, X_WIDTH, D_MODEL), X_WIDTH ** -0.5)
    inp['norm_ffn'] = gain((DEPTH, D_MODEL))
    inp['peer_wq'] = nrm((DEPTH, D_MODEL, P_HEADS * P_DKEY), D_MODEL ** -0.5)
    inp['peer_keys'] = nrm((DEPTH, 2, P_HEADS, P_NKEYS, P_DKEY // 2), (P_DKEY // 2) ** -0.5)
    inp['peer_u'] = nrm((DEPTH, P_EXPERTS, D_MODEL), D_MODEL ** -0.5)
    inp['peer_v'] = nrm((DEPTH, P_EXPERTS, D_MODEL), P_HEADS ** -0.5)
    return inp

def reference(x_prompt, x_sample, cache_k, cache_v, cache_mem_k, cache_mem_v, state_conv, state_ssm,
              page_table, mem_prompt, norm_mix, w_in, q_norm, k_norm, lambda_q1, lambda_k1, lambda_q2,
              lambda_k2, subln, conv_w, conv_b, dt_bias, a_log, d_skip, ssm_norm, w_out, norm_x, norm_mem,
              wq_x, wk_x, wv_x, qx_norm, kx_norm, wo_x, norm_ffn, peer_wq, peer_keys, peer_u, peer_v):
    bp = x_prompt.shape[0]
    bs = x_sample.shape[0]
    yp, ys = x_prompt, x_sample
    kp_l, vp_l, cp_l, sp_l, mkp_l, mvp_l = [], [], [], [], [], []
    ks_l, vs_l, cs_l, ss_l = [], [], [], []
    for l in range(DEPTH):
        lw = dict(norm_mix=norm_mix[l], w_in=w_in[l], q_norm=q_norm[l], k_norm=k_norm[l],
                  lambda_q1=lambda_q1[l], lambda_k1=lambda_k1[l], lambda_q2=lambda_q2[l], lambda_k2=lambda_k2[l],
                  subln=subln[l], conv_w=conv_w[l], conv_b=conv_b[l], dt_bias=dt_bias[l], a_log=a_log[l],
                  d_skip=d_skip[l], ssm_norm=ssm_norm[l], w_out=w_out[l], norm_x=norm_x[l], norm_mem=norm_mem[l],
                  wq_x=wq_x[l], wk_x=wk_x[l], wv_x=wv_x[l], qx_norm=qx_norm[l], kx_norm=kx_norm[l], wo_x=wo_x[l],
                  norm_ffn=norm_ffn[l], peer_wq=peer_wq[l], peer_keys=peer_keys[l], peer_u=peer_u[l], peer_v=peer_v[l])
        mk, mv = memory_kv(mem_prompt, lw)
        conv0 = jnp.zeros((bp, S_CONV - 1, S_CONV_DIM), x_prompt.dtype)
        ssm0 = jnp.zeros((bp, S_HEADS, S_HEAD_DIM, S_STATE), F32)
        yp, kr, vr, cst, sst = decoder_layer(yp, l, lw, mk, mv, conv0, ssm0, None, None)
        kp_l.append(kr); vp_l.append(vr); cp_l.append(cst); sp_l.append(sst); mkp_l.append(mk); mvp_l.append(mv)
        past_k = cache_k[l][page_table].reshape(bs, -1, A_HEADS, 2 * A_DIM)
        past_v = cache_v[l][page_table].reshape(bs, -1, A_HEADS, 2 * A_DIM)
        ys, kr, vr, cst, sst = decoder_layer(ys, l, lw, cache_mem_k[l], cache_mem_v[l], state_conv[l], state_ssm[l], past_k, past_v)
        ks_l.append(kr); vs_l.append(vr); cs_l.append(cst); ss_l.append(sst)
    new_k_prompt = jnp.stack(kp_l)
    new_v_prompt = jnp.stack(vp_l)
    new_conv_prompt = jnp.stack(cp_l)
    new_ssm_prompt = jnp.stack(sp_l)
    new_mem_k_prompt = jnp.stack(mkp_l)
    new_mem_v_prompt = jnp.stack(mvp_l)
    new_k_sample = jnp.stack(ks_l)
    new_v_sample = jnp.stack(vs_l)
    new_conv_sample = jnp.stack(cs_l)
    new_ssm_sample = jnp.stack(ss_l)
    return (yp, ys, new_k_prompt, new_v_prompt, new_conv_prompt, new_ssm_prompt, new_mem_k_prompt,
            new_mem_v_prompt, new_k_sample, new_v_sample, new_conv_sample, new_ssm_sample)


_drawn_inputs = setup_inputs


def setup_inputs(seed=0):
    import zlib

    import numpy as np

    out = dict(_drawn_inputs(seed))
    spreads = {}
    factors = {'q_norm': 3.693,
     'k_norm': 2.795,
     'lambda_q1': 6.326,
     'subln': 3.063,
     'd_skip': 15.367,
     'ssm_norm': 2.882,
     'norm_x': 8.0,
     'norm_mem': 2.802,
     'qx_norm': 6.239,
     'kx_norm': 2.847,
     'norm_ffn': 6.011}
    for name, (base, spread) in spreads.items():
        noise = np.random.default_rng([zlib.crc32(name.encode()), seed]).standard_normal(out[name].shape)
        drawn = base * np.exp(spread * noise) if base else spread * noise
        out[name] = __import__('jax').numpy.asarray(drawn.astype(out[name].dtype))
    for name, factor in factors.items():
        out[name] = (out[name] * factor).astype(out[name].dtype)
    return out
```

```python
from contextlib import ExitStack

import numpy as np

import concourse.bass as bass
from concourse import mybir

F32 = mybir.dt.float32
I32 = mybir.dt.int32
U32 = mybir.dt.uint32
ALU = mybir.AluOpType
ACT = mybir.ActivationFunctionType
AX_X = mybir.AxisListType.X

P = 128
D = 2048
DC = D // P
TP = 512
TS = 8
T = TP + TS
HT = T // 2
NB = TP // P
AH, AD = 8, 64
SH, SP_, SN, SG = 16, 64, 128, 2
SI = SH * SP_
NM = 256
XH, XD = 4, 128
XW = XH * XD
PH, PK, TOPK = 8, 128, 16
PAGE, PAGES = 128, 4
EPS = 1e-6
S_CONV = 4
LAMBDA0 = 0.2
NEG = -1e30
A_SCALE = AD ** -0.5
X_SCALE = XD ** -0.5
CD = SI + 2 * SG * SN
CT = CD // P

RING = 4
STREAM = [
    ("qkv", AH, (0, 1, 2), (0, 1, 0)),
    ("bc", 1, (3, 0, 1, 2), (0, 1, 0, 1)),
    ("zx", SH // 2, (3, 0), (0, 1)),
    ("out", DC // 4, (1, 2, 3, 0), (0, 1, 0, 1)),
    ("mem", XH, (1, 2, 3), (0, 1, 0)),
    ("wo", 1, (0, 1, 2, 3), (0, 1, 0, 1)),
    ("peer", PH // 2, (0, 1), (0, 1)),
]


def stream_places():
    places, tile, loads, uses = {}, 0, [0] * RING, [0, 0]
    for name, runs, slots, pairs in STREAM:
        places[name] = (tile, tuple(loads), tuple(uses), runs, slots, pairs)
        for _ in range(runs):
            for s in slots:
                loads[s] += 1
            tile += len(slots)
        if name == "wo":
            uses = [u + DC // 2 for u in uses]
        else:
            for p in pairs:
                uses[p] += runs
    return places, tile


N_IN = 4
PLACES, N_TILES = stream_places()

PARAMS = dict(norm_mix=DC, norm_x=DC, norm_mem=DC, norm_ffn=DC, q_norm=1, k_norm=1, subln=1, qx_norm=1,
              kx_norm=1, conv_w=CT * 4, conv_b=CT, dt_bias=1, a_log=1, d_skip=SH // 2, ssm_norm=SH // 2,
              lambdas=4 * AD)
CONSTS = dict(ident=P, ones=P, map_ones=P, causal=P, keep=P, even=P, odd=P, pair=P, pair_rows=SH // 2,
              iota=TOPK, eye8=TS * TS)


def offsets(widths):
    at, out = 0, {}
    for name, n in widths.items():
        out[name] = (at, at + n)
        at += n
    return out, at


PARAM_AT, N_PARAM = offsets(PARAMS)
CONST_AT, N_CONST = offsets(CONSTS)


def hold(eng, sem, value):
    if isinstance(value, int) and value <= 0:
        return
    eng.wait_ge(sem, value)


def hold_alone(eng, sem, value, beat):
    if isinstance(value, int):
        hold(eng, sem, value)
        return
    eng.wait_ge(sem, value)
    eng.sem_inc(beat, 1)


class Order:

    def __init__(self, eng, sem):
        self.eng, self.sem, self.n = eng, sem, 0

    def step(self, ins):
        self.n += 1
        ins.then_inc(self.sem, 1)
        self.eng.wait_ge(self.sem, self.n)

    def tell(self, ins, sem, count):
        ins.then_inc(sem, 1)
        self.eng.wait_ge(sem, count)

    def last(self, ins):
        self.n += 1
        ins.then_inc(self.sem, 1)

    def settle(self):
        if self.n:
            self.eng.wait_ge(self.sem, self.n)

    def enter(self):
        self.eng.sem_clear(self.sem)
        self.n = 0


def decoder_step(nc, a):
    ctx = ExitStack()
    with ctx:
        def sb(name, shape, dt=F32):
            return ctx.enter_context(nc.sbuf_tensor(name, shape, dt))

        def sem(name):
            return ctx.enter_context(nc.semaphore(name))

        x = sb("x", [P, DC, T])
        h = sb("h", [P, DC, T])
        mix = sb("mix", [P, DC, T])
        ring = sb("ring", [P, RING, DC * P])
        par = sb("par", [P, N_PARAM])
        con = sb("con", [P, N_CONST])
        lam = sb("lam", [P, 4])
        lamw = sb("lamw", [P, 2 * AD])
        sub8 = sb("sub8", [P, 1])
        ARENA = 17450
        arena = sb("arena", [P, ARENA])
        qs = sb("qs", [P, AH, TS])
        ks = sb("ks", [P, AH, TS])
        vs = sb("vs", [P, AH, TS])

        wdt = sb("wdt", [P, DC * SH])
        table = sb("table", [1, TS * PAGES], I32)
        xa = x[:, :, :].rearrange("p a b -> p (a b)")

        def carve(at, *shape, of=None):
            n = int(np.prod(shape))
            v = (arena if of is None else of)[:, at:at + n]
            if len(shape) == 2:
                v = v.rearrange("p (a b) -> p a b", b=shape[1])
            elif len(shape) == 3:
                v = v.rearrange("p (a b c) -> p a b c", b=shape[1], c=shape[2])
            return v, at + n

        def pr(name, k=0, n=1):
            return par[:, PARAM_AT[name][0] + k:PARAM_AT[name][0] + k + n]

        def co(name, rows=P):
            return con[0:rows, CONST_AT[name][0]:CONST_AT[name][1]]

        ident, ones = co("ident"), co("ones")

        pj = ctx.enter_context(nc.psum_tensor("pj", [P, 2, 2, 512], F32))
        pst = ctx.enter_context(nc.psum_tensor("pst", [P, 2, 512], F32))
        ptr = ctx.enter_context(nc.psum_tensor("ptr", [P, 512], F32))
        pov = ctx.enter_context(nc.psum_tensor("pov", [P, 512], F32))

        def pair(b):
            return pj[:, b, :, 0:HT]

        def halves(v):
            return v.rearrange("p (a t) -> p a t", t=HT)

        s_in = sem("s_in")
        s_loaded = [sem(f"s_loaded{i}") for i in range(RING)]
        s_tile = sem("s_tile")
        s_read = [sem(f"s_read{i}") for i in range(2)]
        s_dve = sem("s_dve")
        s_act = sem("s_act")
        s_beat = sem("s_beat")
        s_out = sem("s_out")
        s_xpart = [sem(f"s_xpart{i}") for i in range(4)]
        s_sqa = sem("s_sqa")
        s_sq = sem("s_sq")
        s_sqsum = sem("s_sqsum")
        s_var = sem("s_var")
        s_root = sem("s_root")
        s_h = sem("s_h")
        s_dve_lam = sem("s_dve_lam")
        s_lam = sem("s_lam")

        nsq, at = carve(0, 2, T)
        nrt, at = carve(at, T)
        nrstd, at = carve(at, T)
        sq, nsum = nsq[:, 0, :], nsq[:, 1, :]

        def first_norm_act(act):
            for j in range(DC // 2):
                if j % 2 == 0:
                    act.wait_ge(s_xpart[j // 2], 16)
                hold(act, s_sqsum, j - 1)
                act.activation((nrt, nrstd)[j % 2], x[:, 2 * j + 1, :], ACT.Square).then_inc(s_sqa, 1)

        def first_norm_dve(dve, o):
            for j in range(DC // 2):
                if j % 2 == 0:
                    dve.wait_ge(s_xpart[j // 2], 16)
                hold(dve, s_sqsum, j - 1)
                o.step(dve.tensor_tensor(nsq[:, j % 2, :], x[:, 2 * j, :], x[:, 2 * j, :], ALU.mult))
                dve.wait_ge(s_sqa, j + 1)
                dve.tensor_tensor(nsq[:, j % 2, :], nsq[:, j % 2, :], (nrt, nrstd)[j % 2], ALU.add).then_inc(s_sq, 1)

        def first_norm_pe(pe):
            for j in range(DC // 2):
                pe.wait_ge(s_sq, j + 1)
                for b in range(2):
                    m = pe.matmul(pst[:, b, 0:HT], ones, nsq[:, j % 2, b * HT:(b + 1) * HT],
                                  start=(j == 0), stop=(j == DC // 2 - 1))
                m.then_inc(s_sqsum, 1)

        def norm_act(act, k, cols):
            act.wait_ge(s_var, k + 1)
            act.activation(nrt[:, 0:cols], nrt[:, 0:cols], ACT.Sqrt).then_inc(s_root, 1)

        def norm_pe(pe, k, sums, cols):
            half = cols // 2
            pe.wait_ge(s_sq, DC // 2 + k)
            pe.wait_ge(s_var, k)
            for b in range(2):
                m = pe.matmul(pst[:, b, 0:half], ones, sums[:, b * half:(b + 1) * half], start=True, stop=True)
            m.then_inc(s_sqsum, 1)

        def norm_dve(dve, o, k, src, dst, gain, cols):
            half = cols // 2
            dve.wait_ge(s_sqsum, DC // 2 + k)
            dve.tensor_scalar(nrt[:, 0:cols].rearrange("p (a t) -> p a t", t=half), pst[:, :, 0:half],
                              1.0 / D, EPS, ALU.mult, ALU.add).then_inc(s_var, 1)
            dve.wait_ge(s_root, k + 1)
            o.step(dve.reciprocal(nrstd[:, 0:cols], nrt[:, 0:cols]))
            for c in range(DC):
                dve.scalar_tensor_tensor(out=dst[:, c, :], in0=src[:, c, :], scalar=pr(gain, c),
                                         in1=nrstd[:, 0:cols], op0=ALU.mult, op1=ALU.mult).then_inc(s_h, 1)

        def add_chunk(dve, o, c, pb):
            xc = x[:, bass.ds(c, 1), :]
            o.step(dve.tensor_tensor(xc.rearrange("p a (b t) -> p (a b) t", t=HT), pair(pb),
                                     xc.rearrange("p a (b t) -> p (a b) t", t=HT), ALU.add))
            dve.sem_inc(s_read[pb], 1)
            xc = xc.rearrange("p a t -> p (a t)")
            o.step(dve.tensor_tensor(sq, xc, xc, ALU.mult))
            o.step(dve.tensor_tensor(nsum, nsum, sq, ALU.add))

        def ready_tile(pe, stage, i, j, pb):
            tile0, loads, uses, runs, slots, pairs = PLACES[stage]
            s = slots[j]
            pe.wait_ge(s_loaded[s], 16 * (loads[s] + i + 1))
            per = pairs.count(pb)
            hold(pe, s_read[pb], uses[pb] + i * per + pairs[:j].count(pb))

        def project(pe, slot, pb, src, c0, c1, cols=T, after=None):
            half = cols // 2
            for c in range(c0, c1):
                if after:
                    pe.wait_ge(after[0], max(1, after[1] + c))
                w = ring[:, slot, c * P:(c + 1) * P]
                if cols == NM:
                    m = pe.matmul(pj[:, pb, 0, 0:NM], w, src[:, c, :], start=(c == 0), stop=(c == DC - 1))
                    continue
                for b in range(2):
                    m = pe.matmul(pj[:, pb, b, 0:half], w, src[:, c, b * half:(b + 1) * half],
                                  start=(c == 0), stop=(c == DC - 1))
            if c1 == DC:
                m.then_inc(s_tile, 1)

        def tile_no(stage, i, j):
            wo = len(PLACES["wo"][4]) if stage == "peer" else 0
            return PLACES[stage][0] - wo + i * len(PLACES[stage][4]) + j

        def read_no(stage, i, j):
            _, _, uses, _, _, pairs = PLACES[stage]
            pb = pairs[j]
            return uses[pb] + i * pairs.count(pb) + pairs[:j].count(pb) + 1

        def uses_of(stage, pb):
            _, _, uses, runs, _, pairs = PLACES[stage]
            return uses[pb] + (DC // 2 if stage == "wo" else runs * pairs.count(pb))

        raw, at = carve(0, 3, T)
        qn, at = carve(at, T)
        kn, at = carve(at, T)
        sq2, at = carve(at, 2, T)
        rt2, at = carve(at, 2, T)
        prob, at = carve(at, 2, TP)
        amix, at = carve(at, TP)
        amixT, at = carve(at, NB, P)
        vnat, at = carve(at, NB, P)
        osq, at = carve(at, TP)
        ort, at = carve(at, TP)
        assert at <= ARENA, at
        negmax = sb("negmax", [P, 2])
        dsum = sb("dsum", [P, 2])
        drec = sb("drec", [P, 2])

        s_vT = sem("s_vT")
        s_vnat = sem("s_vnat")
        s_score = sem("s_score")
        s_shift = sem("s_shift")
        s_exp = sem("s_exp")
        s_mixed = sem("s_mixed")
        s_mixT = sem("s_mixT")
        s_mixTc = sem("s_mixTc")
        s_pv = sem("s_pv")
        s_qksq = sem("s_qksq")
        s_qksum = sem("s_qksum")
        s_qkvar = sem("s_qkvar")
        s_qkroot = sem("s_qkroot")
        s_qn = sem("s_qn")
        s_kn = sem("s_kn")
        s_osq = sem("s_osq")
        s_osum = sem("s_osum")
        s_ovar = sem("s_ovar")
        s_oroot = sem("s_oroot")
        s_omix = sem("s_omix")
        s_kout = sem("s_kout")
        s_qs = sem("s_qs")

        def attention_pe(pe, g, do_proj, do_att):
            def quarter(j, n, slot, pb):
                if do_proj:
                    if n == 0:
                        ready_tile(pe, "qkv", g, j, pb)
                    project(pe, slot, pb, h, 4 * n, 4 * n + 4,
                            after=(s_h, 1) if do_att is False and j == 0 else None)

            def values():
                pe.wait_ge(s_read[0], read_no("qkv", g - 1, 2))
                hold(pe, s_mixTc, 4 * (g - 1))
                for b in range(NB):
                    m = pe.transpose(ptr[:, b * P:(b + 1) * P], raw[:, 2, b * P:(b + 1) * P], ident)
                m.then_inc(s_vT, 1)

            def scores(b):
                if b == 0:
                    pe.wait_ge(s_qn, g)
                    pe.wait_ge(s_kn, g)
                hold(pe, s_exp, 4 * (g - 1) + b)
                n = (b + 1) * P
                for m in range(2):
                    r = slice(m * AD, (m + 1) * AD)
                    mm = pe.matmul(pst[:, m, 0:n], qn[r, b * P:(b + 1) * P], kn[r, 0:n], start=True, stop=True)
                mm.then_inc(s_score, 1)

            def transposes(b):
                pe.wait_ge(s_mixed, 4 * (g - 1) + b + 1)
                if b == 0:
                    pe.wait_ge(s_vnat, g)
                else:
                    pe.wait_ge(s_mixTc, 4 * (g - 1) + b)
                for kb in range(b + 1):
                    m = pe.transpose(ptr[:, kb * P:(kb + 1) * P], amix[:, kb * P:(kb + 1) * P], ident)
                m.then_inc(s_mixT, 1)

            def pv(b):
                pe.wait_ge(s_mixTc, 4 * (g - 1) + b + 1)
                if b == 0:
                    hold(pe, s_omix, g - 1)
                for kb in range(b + 1):
                    m = pe.matmul(pov[:, b * P:(b + 1) * P], vnat[:, kb, :], amixT[:, kb, :],
                                  start=(kb == 0), stop=(kb == b))
                m.then_inc(s_pv, 1)

            def qk_sums(j):
                pe.wait_ge(s_qksq, 2 * g + j + 1)
                pe.wait_ge(s_qkvar, 2 * g + j) if j else hold(pe, s_ovar, g - 1)
                if j == 0:
                    hold(pe, s_exp, 4 * g)
                for b in range(2):
                    m = pe.matmul(pst[:, b, 0:HT], co("map_ones"), sq2[:, j, b * HT:(b + 1) * HT],
                                  start=True, stop=True)
                m.then_inc(s_qksum, 1)

            def out_sums():
                pe.wait_ge(s_osq, g)
                pe.matmul(ptr[:, :], ones, osq, start=True, stop=True).then_inc(s_osum, 1)

            quarter(0, 0, 0, 0)
            if do_att:
                values()
                scores(0)
            quarter(0, 1, 0, 0)
            if do_att:
                transposes(0)
                scores(1)
            quarter(0, 2, 0, 0)
            if do_att:
                pv(0)
                transposes(1)
                scores(2)
            quarter(0, 3, 0, 0)
            if do_att:
                pv(1)
                transposes(2)
                scores(3)
            quarter(1, 0, 1, 1)
            if do_att:
                pv(2)
                transposes(3)
            quarter(1, 1, 1, 1)
            if do_att:
                pv(3)
            quarter(1, 2, 1, 1)
            if do_proj:
                qk_sums(0)
            quarter(1, 3, 1, 1)
            if do_att:
                out_sums()
            quarter(2, 0, 2, 0)
            quarter(2, 1, 2, 0)
            if do_proj:
                qk_sums(1)
            quarter(2, 2, 2, 0)
            quarter(2, 3, 2, 0)

        def attention_act(act, o, g, do_proj, do_att):
            def exps(b):
                act.wait_ge(s_shift, 4 * (g - 1) + b + 1)
                n = (b + 1) * P
                hold(act, s_mixed, 4 * (g - 1) + b)
                o.last(act.activation(prob[:, 0, 0:n], pst[:, 0, 0:n], ACT.Exp, bias=negmax[:, 0:1],
                                      scale=A_SCALE, accum_out=dsum[:, 0:1]))
                act.activation(prob[:, 1, 0:n], pst[:, 1, 0:n], ACT.Exp, bias=negmax[:, 1:2],
                               scale=A_SCALE, accum_out=dsum[:, 1:2]).then_inc(s_exp, 1)

            def copy_map(b):
                act.wait_ge(s_mixT, 4 * (g - 1) + b + 1)
                hold(act, s_pv, 4 * (g - 1) + b)
                n = (b + 1) * P
                act.activation(amixT[:, 0:b + 1, :], ptr[:, 0:n].rearrange("p (a t) -> p a t", t=P),
                               ACT.Copy).then_inc(s_mixTc, 1)

            def copy_out(j):
                pb = PLACES["qkv"][5][j]
                act.wait_ge(s_tile, tile_no("qkv", g, j) + 1)
                if j < 2:
                    hold(act, (s_qn, s_kn)[j], g)
                else:
                    hold(act, s_vnat, g)
                    hold(act, s_kout, 32 * g)
                    hold(act, s_qs, g)
                o.tell(act.activation(halves(raw[:, j, :]), pair(pb), ACT.Copy), s_read[pb],
                         read_no("qkv", g, j))

            def squares(j):
                act.activation(sq2[:, j, :], raw[:, j, :], ACT.Square).then_inc(s_qksq, 1)

            def roots():
                for j in range(2):
                    act.wait_ge(s_qkvar, 2 * g + j + 1)
                    act.activation(rt2[:, j, :], rt2[:, j, :], ACT.Sqrt).then_inc(s_qkroot, 1)

            if do_att:
                act.wait_ge(s_vT, g)
                hold(act, s_pv, 4 * (g - 1))
                act.activation(vnat[:, :, :], ptr[:, :].rearrange("p (a t) -> p a t", t=P),
                               ACT.Copy).then_inc(s_vnat, 1)
                exps(0)
                copy_map(0)
                exps(1)
                copy_map(1)
                exps(2)
                copy_map(2)
                exps(3)
            if do_proj:
                copy_out(0)
                squares(0)
            if do_att:
                copy_map(3)
                act.wait_ge(s_pv, 4 * g)
                act.activation(osq, pov[:, :], ACT.Square).then_inc(s_osq, 1)
            if do_proj:
                copy_out(1)
                squares(1)
            if do_att:
                act.wait_ge(s_ovar, g)
                act.activation(ort, ort, ACT.Sqrt).then_inc(s_oroot, 1)
            if do_proj:
                roots()
                copy_out(2)

        def attention_dve(dve, o, g, do_proj, do_att):
            def block(b):
                n = (b + 1) * P
                dve.wait_ge(s_score, 4 * (g - 1) + b + 1)
                diag = pst[:, :, b * P:n]
                o.step(dve.tensor_tensor(diag, diag, co("causal")[:, None, :].broadcast_to([P, 2, P]), ALU.add))
                o.step(dve.tensor_reduce(negmax[:, :], pst[:, :, 0:n], AX_X, ALU.max))
                dve.tensor_scalar(negmax[:, :], negmax[:, :], -A_SCALE, None, ALU.mult).then_inc(s_shift, 1)
                dve.wait_ge(s_exp, 4 * (g - 1) + b + 1)
                o.step(dve.reciprocal(drec[:, :], dsum[:, :]))
                o.step(dve.tensor_scalar(drec[:, 1:2], drec[:, 1:2], lam[:, 1:2], None, ALU.mult))
                hold(dve, s_mixT, 4 * (g - 1) + b)
                o.step(dve.tensor_scalar(amix[:, 0:n], prob[:, 0, 0:n], drec[:, 0:1], None, ALU.mult))
                o.tell(dve.scalar_tensor_tensor(out=amix[:, 0:n], in0=prob[:, 1, 0:n], scalar=drec[:, 1:2],
                                                  in1=amix[:, 0:n], op0=ALU.mult, op1=ALU.add),
                         s_mixed, 4 * (g - 1) + b + 1)

            def mean_square(j):
                dve.wait_ge(s_qksum, 2 * g + j + 1)
                dve.tensor_scalar(halves(rt2[:, j, :]), pst[:, :, 0:HT], 1.0 / AD, EPS, ALU.mult,
                                  ALU.add).then_inc(s_qkvar, 1)

            def normed(j, dst, gain, s):
                dve.wait_ge(s_qkroot, 2 * g + j + 1)
                o.step(dve.reciprocal(rt2[:, j, :], rt2[:, j, :]))
                if j == 0:
                    hold(dve, s_score, 4 * g)
                else:
                    hold(dve, s_kout, 32 * g)
                o.tell(dve.scalar_tensor_tensor(out=dst, in0=raw[:, j, :], scalar=gain, in1=rt2[:, j, :],
                                                  op0=ALU.mult, op1=ALU.mult), s, g + 1)

            if do_att:
                for b in range(NB):
                    block(b)
            if do_proj:
                mean_square(0)
            if do_att:
                dve.wait_ge(s_osum, g)
                dve.tensor_scalar(ort, ptr[:, :], 1.0 / P, EPS, ALU.mult, ALU.add).then_inc(s_ovar, 1)
                dve.wait_ge(s_oroot, g)
                o.step(dve.reciprocal(ort, ort))
                dve.scalar_tensor_tensor(out=mix[:, bass.ds(g - 1, 1), 0:TP].rearrange("p a t -> p (a t)"),
                                         in0=pov[:, :], scalar=sub8[:, 0:1], in1=ort, op0=ALU.mult,
                                         op1=ALU.mult).then_inc(s_omix, 1)
            if do_proj:
                mean_square(1)
                normed(0, qn, pr("q_norm"), s_qn)
                normed(1, kn, pr("k_norm"), s_kn)
                for dst, src in ((qs, qn), (ks, kn)):
                    o.last(dve.tensor_copy(dst[:, bass.ds(g, 1), :].rearrange("p a t -> p (a t)"), src[:, TP:T]))
                dve.wait_ge(s_read[0], read_no("qkv", g, 2))
                dve.tensor_copy(vs[:, bass.ds(g, 1), :].rearrange("p a t -> p (a t)"),
                                raw[:, 2, TP:T]).then_inc(s_qs, 1)

        def attention_stores(pool, g):
            hold_alone(pool, s_kn, g + 1, s_beat)
            pool.dma_start(a["k_out"][bass.ds(g, 1)].rearrange("a p t -> p (a t)"), kn).then_inc(s_kout, 16)
            hold_alone(pool, s_read[0], read_no("qkv", g, 2), s_beat)
            pool.dma_start(a["v_out"][bass.ds(g, 1)].rearrange("a p t -> p (a t)"),
                           raw[:, 2, :]).then_inc(s_kout, 16)

        bc, at = carve(0, 4, T, of=xa)
        rows, at = carve(at, 2, TS * SN, of=xa)
        kv, at = carve(at, PAGES, AH * 2 * AD, of=xa)
        assert at <= DC * T, at
        gt, at = carve(0, SG, NB, P)
        bnat, at = carve(at, SG, NB, P)
        xraw, at = carve(at, T)
        xs, at = carve(at, T)
        zg, at = carve(at, T)
        xd, at = carve(at, TP)
        xn, at = carve(at, NB, P)
        xdec = xd.rearrange("p (a b) -> p a b", b=P)
        dec, at = carve(at, 2, TP)
        gap, at = carve(at, 2, TP)
        cdec, at = carve(at, 2, TP)
        hst, at = carve(at, NB + 1, P)
        dts, at = carve(at, T)
        acs, at = carve(at, T)
        dtw, at = carve(at, T)
        yv = dtw
        dtp, at = carve(at, 2, T)
        cols, at = carve(at, 2, NB, SH)
        prev, at = carve(at, CT, (S_CONV - 1) * TS)
        tails, at = carve(at, CT, (S_CONV - 1) * TS)
        tailp, at = carve(at, CT, S_CONV - 1)
        qnat, at = carve(at, AH * 2 * AD)
        qmask, at = carve(at, AH * 2 * AD)
        qrow, at = carve(at, AH * 2 * AD)
        prod, at = carve(at, AH * 2 * AD)
        state, at = carve(at, TS * SN)
        small, at = carve(at, 640)
        assert at <= ARENA, at
        cflat = cols[:, :, :, :].rearrange("p a b c -> p (a b c)")
        gflat = gt[:, :, :, :].rearrange("p a b c -> p (a b c)")
        s_hout = sem("s_hout")
        knew = small[:, 0:128].rearrange("p (b n) -> p b n", n=16)
        s5 = small[:, 128:208].rearrange("p (k n) -> p k n", n=16)
        m1 = small[:, 208:224]
        mcol = small[:, 224:225]
        mdiag = small[:, 225:241]
        rden = small[:, 241:257]
        a5 = small[:, 260:300].rearrange("p (k n) -> p k n", n=8)
        dsmp = small[:, 300:308]
        xsmp = small[:, 308:316]
        snew = small[:, 316:332]
        sdiag = small[:, 336:464]
        ysmp = small[:, 464:472]
        aneg = small[:, 472:473]
        o64 = sb("o64", [P, AH, TS])
        onew = sb("onew", [P, TS])

        s_dt = sem("s_dt")
        s_dtn = sem("s_dtn")
        s_dta = sem("s_dta")
        s_dtT = sem("s_dtT")
        s_prep = sem("s_prep")
        s_bct = sem("s_bct")
        s_bctc = sem("s_bctc")
        s_nat = sem("s_nat")
        s_natc = sem("s_natc")
        s_new = sem("s_new")
        s_newb = sem("s_newb")
        s_rowT = sem("s_rowT")
        s_rowd = sem("s_rowd")
        s_rowb = sem("s_rowb")
        s_rowc = sem("s_rowc")
        s_conv = sem("s_conv")
        s_silu = sem("s_silu")
        s_pairs = sem("s_pairs")
        s_bcast = sem("s_bcast")
        s_decay = sem("s_decay")
        s_gapd = sem("s_gapd")
        s_gape = sem("s_gape")
        s_x = sem("s_x")
        s_xT = sem("s_xT")
        s_xTc = sem("s_xTc")
        s_xdec = sem("s_xdec")
        s_state = sem("s_state")
        s_hst = sem("s_hst")
        s_y = sem("s_y")
        s_ymix = sem("s_ymix")
        s_qm = sem("s_qm")
        s_qrow = sem("s_qrow")
        s_qrowc = sem("s_qrowc")
        s_page = [sem(f"s_page{k}") for k in range(PAGES)]
        s_prod = sem("s_prod")
        s_m1 = sem("s_m1")
        s_m1T = sem("s_m1T")
        s_mdiag = sem("s_mdiag")
        s_mrow = sem("s_mrow")
        s_sh = sem("s_sh")
        s_pe5 = sem("s_pe5")
        s_den = sem("s_den")
        s_a5 = sem("s_a5")
        s_opv = sem("s_opv")
        s_opvc = sem("s_opvc")
        s_oT = sem("s_oT")
        s_o64 = sem("s_o64")
        s_st = sem("s_st")
        s_stn = sem("s_stn")
        s_stout = sem("s_stout")
        s_tails = sem("s_tails")
        s_prev = sem("s_prev")
        s_osn = sem("s_osn")
        s_osn_a = sem("s_osn_a")
        s_osn_p = sem("s_osn_p")
        s_ysq = sem("s_ysq")
        s_ysum = sem("s_ysum")
        s_yvar = sem("s_yvar")
        s_yroot = sem("s_yroot")
        s_mixed_all = sem("s_mixed_all")

        def convolve(o, dve, ct, dst):
            def w(k):
                return par[:, bass.ds(ct * 4 + (PARAM_AT["conv_w"][0] + k), 1)]
            bias = par[:, bass.ds(ct + PARAM_AT["conv_b"][0], 1)]
            o.step(dve.tensor_scalar(dst, xraw, w(3), bias, ALU.mult, ALU.add))
            pv = prev[:, bass.ds(ct, 1), :].rearrange("p a n -> p (a n)")
            for k in range(1, 4):
                o.step(dve.scalar_tensor_tensor(out=dst[:, k:TP], in0=xraw[:, 0:TP - k], scalar=w(3 - k),
                                                in1=dst[:, k:TP], op0=ALU.mult, op1=ALU.add))
                o.step(dve.scalar_tensor_tensor(out=dst[:, TP:T], in0=pv[:, (3 - k) * TS:(4 - k) * TS],
                                                scalar=w(3 - k), in1=dst[:, TP:T], op0=ALU.mult, op1=ALU.add))
            o.last(dve.tensor_scalar(tails[:, bass.ds(ct, 1), 2 * TS:3 * TS].rearrange("p a n -> p (a n)"),
                                     xraw[:, TP:T], 0.0, None, ALU.add))
            dve.tensor_scalar(tailp[:, bass.ds(ct, 1), :].rearrange("p a n -> p (a n)"),
                              xraw[:, TP - 3:TP], 0.0, None, ALU.add).then_inc(s_conv, 1)

        def prepare_pe(pe):
            for c in range(DC):
                for b in range(2):
                    m = pe.matmul(pst[0:SH, b, 0:HT], wdt[:, c * SH:(c + 1) * SH], h[:, c, b * HT:(b + 1) * HT],
                                  start=(c == 0), stop=(c == DC - 1))
            m.then_inc(s_dt, 1)
            for j in range(4):
                pb = j % 2
                ready_tile(pe, "bc", 0, j, pb)
                project(pe, PLACES["bc"][4][j], pb, h, 0, DC)
            pe.wait_ge(s_dta, 4)
            for k, src in enumerate((acs, dtw)):
                for b in range(NB):
                    m = pe.transpose(ptr[:, (k * NB + b) * SH:(k * NB + b + 1) * SH], src[0:SH, b * P:(b + 1) * P],
                                     ident[0:SH, 0:SH])
            m.then_inc(s_dtT, 1)
            for k, src in enumerate((qs, ks)):
                pe.wait_ge(s_natc, k) if k else pe.wait_ge(s_qs, AH)
                for n in range(AH):
                    m = pe.transpose(pst[0:TS, n // 4, (n % 4) * P:(n % 4 + 1) * P], src[:, n, :], ident)
                m.then_inc(s_nat, 1)
            for g in range(SG):
                pe.wait_ge(s_silu, 4)
                if g == 0:
                    pe.wait_ge(s_natc, 2)
                    pe.wait_ge(s_dtn, 6)
                else:
                    pe.wait_ge(s_bctc, 1)
                for b in range(NB):
                    pe.matmul(pov[:, b * P:(b + 1) * P], bc[:, g, b * P:(b + 1) * P],
                              bc[:, 2 + g, b * P:(b + 1) * P], start=True, stop=True)
                for b in range(NB):
                    m = pe.transpose(ptr[:, b * P:(b + 1) * P], bc[:, g, b * P:(b + 1) * P], ident)
                m.then_inc(s_bct, 1)
            pe.wait_ge(s_new, 1)
            pe.matmul(pst[:, 0, 0:P], ones[0:TS, :], sdiag[0:TS, :], start=True, stop=True).then_inc(s_newb, 1)

        def group_pe(pe, g):
            for k in range(2):
                if g == 0 and k == 0:
                    pe.wait_ge(s_prep, 1)
                else:
                    pe.wait_ge(s_rowc, 2 * g + k)
                if g:
                    pe.wait_ge(s_o64, NB)
                pe.transpose(pov[0:TS, 0:P], bc[:, 2 * k + g, TP:T], ident).then_inc(s_rowT, 1)
                pe.wait_ge(s_rowd, 2 * g + k + 1)
                for b in range(2):
                    m = pe.matmul(pst[:, b, :], ones[0:TS, :], qmask[0:TS, b * 512:(b + 1) * 512],
                                  start=True, stop=True)
                m.then_inc(s_rowb, 1)

        def group_dve(dve, o, g):
            for k in range(2):
                dve.wait_ge(s_rowT, 2 * g + k + 1)
                if k == 0 and g:
                    dve.wait_ge(s_stn, NB)
                    dve.wait_ge(s_qrow, NB)
                if k:
                    dve.wait_ge(s_rowb, 2 * g + k)
                dve.tensor_tensor(qmask[0:TS, :].rearrange("p (b n) -> p b n", n=SN),
                                  pov[0:TS, 0:P][:, None, :].broadcast_to([TS, TS, SN]),
                                  ident[0:TS, 0:TS][:, :, None].broadcast_to([TS, TS, SN]),
                                  ALU.mult).then_inc(s_rowd, 1)

        def group_act(act, g):
            for k in range(2):
                act.wait_ge(s_rowb, 2 * g + k + 1)
                if g:
                    act.wait_ge(s_stn, NB)
                act.activation(rows[:, k, :], pst[:, :, :].rearrange("p a b -> p (a b)"), ACT.Copy).then_inc(s_rowc, 1)

        def prepare_act(act, o):
            act.wait_ge(s_dtn, 2)
            act.activation(dtw[0:SH, :], dtw[0:SH, :], ACT.Exp, scale=-1.0).then_inc(s_dta, 1)
            act.activation(aneg[0:SH, :], pr("a_log")[0:SH, :], ACT.Exp).then_inc(s_dta, 1)
            act.wait_ge(s_dta, 2)
            act.activation(dtw[0:SH, :], dtw[0:SH, :], ACT.Ln, bias=1.0).then_inc(s_dta, 1)
            act.wait_ge(s_dtn, 5)
            act.activation(dtw[0:SH, 0:TP], dtw[0:SH, 0:TP], ACT.Exp).then_inc(s_dta, 1)
            for j in range(4):
                pb = j % 2
                act.wait_ge(s_tile, tile_no("bc", 0, j) + 1)
                hold(act, s_conv, j)
                act.activation(halves(xraw), pair(pb), ACT.Copy).then_inc(s_read[pb], 1)
                act.wait_ge(s_conv, j + 1)
                act.activation(bc[:, j, :], bc[:, j, :], ACT.Silu).then_inc(s_silu, 1)
            for k, dst in enumerate((qnat, qmask)):
                act.wait_ge(s_nat, k + 1)
                act.activation(dst[0:TS, :], pst[0:TS, :, :].rearrange("p a b -> p (a b)"),
                               ACT.Copy).then_inc(s_natc, 1)

        def prepare_dve(dve, o):
            r = slice(0, SH)
            dve.wait_ge(s_omix, AH)
            dve.wait_ge(s_kout, 32 * AH)
            dve.wait_ge(s_prev, 16)
            o.step(dve.tensor_copy(tails[:, :, 0:2 * TS], prev[:, :, TS:3 * TS]))
            dve.wait_ge(s_dt, 1)
            dve.tensor_scalar(halves(dts)[r], pst[r, :, 0:HT], pr("dt_bias")[r], None, ALU.add).then_inc(s_dtn, 1)
            dve.wait_ge(s_dtn, 1)
            dve.scalar_tensor_tensor(out=dtw[r], in0=dts[r], scalar=-1.0, in1=dts[r], op0=ALU.mult,
                                     op1=ALU.max).then_inc(s_dtn, 1)
            dve.wait_ge(s_dta, 3)
            dve.scalar_tensor_tensor(out=dts[r], in0=dts[r], scalar=0.0, in1=dtw[r], op0=ALU.max,
                                     op1=ALU.add).then_inc(s_dtn, 1)
            dve.wait_ge(s_dtn, 3)
            dve.tensor_scalar(acs[r], dts[r], aneg[r], -1.0, ALU.mult, ALU.mult).then_inc(s_dtn, 1)
            dve.wait_ge(s_dtn, 4)
            for b in range(NB):
                c = slice(b * P, (b + 1) * P)
                o.step(dve.tensor_tensor_scan(dtw[r, c], ones[r, :], acs[r, c], 0.0, ALU.mult, ALU.add))
            o.step(dve.tensor_scalar(acs[r, 0:TP], dtw[r, 0:TP], 0.0, None, ALU.add))
            for b in range(NB):
                c = slice(b * P, (b + 1) * P)
                m = dve.tensor_scalar(dtw[r, c], acs[r, c], -1.0, acs[r, (b + 1) * P - 1:(b + 1) * P],
                                      ALU.mult, ALU.add)
                o.last(m) if b < NB - 1 else m.then_inc(s_dtn, 1)
            for j in range(4):
                dve.wait_ge(s_read[j % 2], read_no("bc", 0, j))
                convolve(o, dve, (SI // P) + j, bc[:, j, :])
            dve.wait_ge(s_dtT, 1)
            dve.tensor_copy(cols[:, :, :, :].rearrange("p a b c -> p (a b c)"), ptr[:, 0:2 * NB * SH]).then_inc(s_dtn, 1)
            dve.wait_ge(s_natc, 2)
            o.step(dve.tensor_tensor(prod[0:TS], qnat[0:TS], qmask[0:TS], ALU.mult))
            o.step(dve.tensor_reduce(snew[0:TS], prod[0:TS].rearrange("p (n d) -> p n d", d=AD), AX_X, ALU.add))
            dve.tensor_tensor(sdiag[0:TS].rearrange("p (b n) -> p b n", n=16),
                              snew[0:TS][:, None, :].broadcast_to([TS, TS, 16]),
                              ident[0:TS, 0:TS][:, :, None].broadcast_to([TS, TS, 16]), ALU.mult).then_inc(s_new, 1)
            for g in range(SG):
                dve.wait_ge(s_bct, g + 1)
                o.last(dve.tensor_tensor(gt[:, g, :, :], pov[:, :].rearrange("p (a b) -> p a b", b=P),
                                         co("keep")[:, None, :].broadcast_to([P, NB, P]), ALU.mult))
                dve.tensor_copy(bnat[:, g, :, :].rearrange("p a b -> p (a b)"), ptr[:, :]).then_inc(s_bctc, 1)
            dve.wait_ge(s_newb, 1)
            dve.tensor_copy(small[:, 0:128], pst[:, 0, 0:P]).then_inc(s_prep, 1)

        def pairs_pe(pe, i, g, proj, ssd):
            s = i - 1

            def quarter(j, n):
                if proj:
                    slot, pb = PLACES["zx"][4][j], j
                    if n == 0:
                        ready_tile(pe, "zx", i, j, pb)
                    project(pe, slot, pb, h, 4 * n, 4 * n + 4)

            quarter(0, 0)
            if ssd:
                pe.wait_ge(s_qm, s + 1)
                pe.wait_ge(s_rowc, 2 * g + 2)
                for b in range(2):
                    m = pe.matmul(pst[:, b, :], ones[0:TS, :], qmask[0:TS, b * 512:(b + 1) * 512], start=True, stop=True)
                m.then_inc(s_qrow, 1)
            quarter(0, 1)
            if ssd:
                pe.wait_ge(s_pairs, s + 1)
                pe.wait_ge(s_qrowc, s + 1)
                hold(pe, s_o64, s)
                hold(pe, s_ymix, s)
                pe.matmul(pov[:, :], co("pair", SH), dtp[0:SH, 0, 0:TP], start=True, stop=True)
                pe.matmul(ptr[:, 0:TS], co("pair", SH), dtp[0:SH, 0, TP:T], start=True, stop=True)
                pe.matmul(ptr[:, TS:2 * TS], co("pair", SH), dtp[0:SH, 1, TP:T], start=True, stop=True)
                pe.matmul(pst[:, 0, :], co("even", SH), dtp[0:SH, 1, 0:TP], start=True, stop=True)
                pe.matmul(pst[:, 1, :], co("odd", SH), dtp[0:SH, 1, 0:TP], start=True, stop=True).then_inc(s_bcast, 1)
            quarter(0, 2)
            if ssd:
                pe.wait_ge(s_x, s + 1)
                pe.wait_ge(s_decay, s + 1)
                for b in range(NB):
                    m = pe.transpose(ptr[:, b * P:(b + 1) * P], xd[:, b * P:(b + 1) * P], ident)
                m.then_inc(s_xT, 1)
                pe.wait_ge(s_m1, s + 1)
                pe.transpose(pov[0:16, 0:P], m1, ident).then_inc(s_m1T, 1)
            quarter(0, 3)
            if ssd:
                pe.wait_ge(s_mdiag, s + 1)
                pe.matmul(pov[:, P:P + 16], ones[0:16, :], mdiag[0:16, :], start=True, stop=True).then_inc(s_mrow, 1)
            quarter(1, 0)
            if ssd:
                pe.wait_ge(s_pe5, s + 1)
                pe.matmul(pov[:, 192:256], ones, s5[:, 0:PAGES, :].rearrange("p a b -> p (a b)"),
                          start=True, stop=True).then_inc(s_den, 1)
            quarter(1, 1)
            if ssd:
                pe.wait_ge(s_xdec, s + 1)
                pe.wait_ge(s_a5, s + 1)
                for b in range(NB):
                    m = pe.matmul(pov[:, b * P:(b + 1) * P], bnat[:, g, b, :], xdec[:, b, :], start=True, stop=True)
                m.then_inc(s_state, 1)
                pe.wait_ge(s_gapd, 2 * s + 2)
                for k in range(PAGES):
                    pe.wait_ge(s_page[k], s * 32 + 32)
                    for b in range(2):
                        m = pe.matmul(pst[0:AH, b, :], a5[:, k, :], kv[:, k, b * 512:(b + 1) * 512],
                                      start=(k == 0), stop=(k == PAGES - 1))
                m.then_inc(s_opv, 1)
                pe.wait_ge(s_hst, s + 1)
                pe.wait_ge(s_xTc, s + 1)
                for e in range(2):
                    r = slice(e * SP_, (e + 1) * SP_)
                    for b in range(NB):
                        c = slice(b * P, (b + 1) * P)
                        m = pe.matmul(ptr[r, c], xn[:, b, r], gap[:, e, c], start=True, stop=(b == 0))
                        if b:
                            m = pe.matmul(ptr[r, c], hst[:, b, r], cdec[:, e, c], start=False, stop=True)
                m.then_inc(s_y, 1)
            quarter(1, 2)
            quarter(1, 3)
            if ssd:
                hold_alone(pe, s_opvc, s + 1, s_beat)
                for n in range(AH):
                    m = pe.transpose(pov[:, 256 + n * AH:256 + (n + 1) * AH], qmask[0:AH, n * P:(n + 1) * P],
                                     ident[0:AH, 0:AH])
                m.then_inc(s_oT, 1)

        def pairs_act(act, o, i, g, proj, ssd):
            s = i - 1
            if ssd:
                hold(act, s_oT, s)
                act.activation(qmask[0:TS, :], qnat[0:TS, :], ACT.Copy,
                               scale=con[0:TS, bass.ds(s + CONST_AT["ident"][0], 1)]).then_inc(s_qm, 1)
                hold(act, s_bcast, s)
                pick = con[0:SH, bass.ds(s + CONST_AT["pair_rows"][0], 1)]
                o.last(act.activation(dtp[0:SH, 0, :], dts[0:SH, :], ACT.Copy, scale=pick))
                act.activation(dtp[0:SH, 1, :], acs[0:SH, :], ACT.Copy, scale=pick).then_inc(s_pairs, 1)
                act.wait_ge(s_qrow, s + 1)
                act.activation(qrow, pst[:, :, :].rearrange("p a b -> p (a b)"), ACT.Copy).then_inc(s_qrowc, 1)
                act.wait_ge(s_bcast, s + 1)
                hold(act, s_ymix, s)
                act.activation(dec[:, :, :], pst[:, :, :], ACT.Exp).then_inc(s_decay, 1)
                act.wait_ge(s_x, s + 1)
                o.last(act.activation(dsmp, dsmp, ACT.Exp))
                for e in range(2):
                    act.wait_ge(s_gapd, 2 * s + e + 1)
                    act.activation(gap[:, e, :], gap[:, e, :], ACT.Exp).then_inc(s_gape, 1)
                act.wait_ge(s_xT, s + 1)
                act.activation(xn[:, :, :].rearrange("p a b -> p (a b)"), ptr[:, :], ACT.Copy).then_inc(s_xTc, 1)
                act.wait_ge(s_sh, s + 1)
                act.activation(s5, s5, ACT.Exp, scale=A_SCALE).then_inc(s_pe5, 1)
            if proj:
                act.wait_ge(s_tile, tile_no("zx", i, 0) + 1)
                act.wait_ge(s_conv, i + 4)
                act.activation(halves(xraw), pair(0), ACT.Copy).then_inc(s_read[0], 1)
            if ssd:
                act.wait_ge(s_opv, s + 1)
                act.activation(qmask[0:AH, :], pst[0:AH, :, :].rearrange("p a b -> p (a b)"), ACT.Copy).then_inc(s_opvc, 1)
            if proj:
                act.wait_ge(s_tile, tile_no("zx", i, 1) + 1)
                hold(act, s_ymix, i)
                act.activation(halves(zg), pair(1), ACT.Silu).then_inc(s_read[1], 1)
                act.wait_ge(s_conv, i + 5)
                act.activation(xs, xs, ACT.Silu).then_inc(s_silu, 1)

        def pairs_dve(dve, o, i, g, proj, ssd):
            s = i - 1
            if ssd:
                dve.wait_ge(s_qrowc, s + 1)
                for k in range(PAGES):
                    dve.wait_ge(s_page[k], s * 32 + 16)
                    o.step(dve.tensor_tensor(prod, kv[:, k, :], qrow, ALU.mult))
                    dve.tensor_reduce(s5[:, k, :], prod.rearrange("p (n d) -> p n d", d=AD), AX_X,
                                      ALU.add).then_inc(s_prod, 1)
                    dve.wait_ge(s_prod, s * 4 + k + 1)
                o.step(dve.tensor_scalar(s5[:, PAGES, :], small[:, bass.ds(s * 16, 16)], 0.0, None, ALU.add))
                dve.tensor_reduce(m1, s5.rearrange("p k n -> p n k"), AX_X, ALU.max).then_inc(s_m1, 1)
                dve.wait_ge(s_bcast, s + 1)
                dve.wait_ge(s_silu, s + 5)
                o.last(dve.tensor_tensor(xsmp, xs[:, TP:T], ptr[:, 0:TS], ALU.mult))
                o.last(dve.tensor_copy(dsmp, ptr[:, TS:2 * TS]))
                dve.tensor_tensor(xd, xs[:, 0:TP], pov[:, :], ALU.mult).then_inc(s_x, 1)
                dve.wait_ge(s_decay, s + 1)
                for e in range(2):
                    for b in range(NB):
                        c = slice(b * P, (b + 1) * P)
                        at0 = b * SH + e
                        m = dve.tensor_scalar(gap[:, e, c], pst[:, e, c], cflat[:, bass.ds(s * 2 + at0, 1)], 0.0,
                                              ALU.subtract, ALU.min)
                        o.last(m) if b < NB - 1 else m.then_inc(s_gapd, 1)
                dve.wait_ge(s_m1T, s + 1)
                o.step(dve.tensor_reduce(mcol[0:16], pov[0:16, 0:P], AX_X, ALU.max))
                dve.tensor_scalar(mdiag[0:16], ident[0:16, 0:16], mcol[0:16], None, ALU.mult).then_inc(s_mdiag, 1)
                o.last(dve.tensor_tensor(cdec[:, :, :], dec[:, :, :],
                                         bc[:, 2 + g, 0:TP][:, None, :].broadcast_to([P, 2, TP]), ALU.mult))
                dve.wait_ge(s_gape, 2 * s + 2)
                o.last(dve.tensor_tensor(gap[:, :, :], gap[:, :, :], gflat[:, None, g * TP:(g + 1) * TP]
                                         .broadcast_to([P, 2, TP]), ALU.mult))
                dve.wait_ge(s_mrow, s + 1)
                dve.tensor_tensor(s5, s5, pov[:, P:P + 16][:, None, :].broadcast_to([P, PAGES + 1, 16]),
                                  ALU.subtract).then_inc(s_sh, 1)
                dve.wait_ge(s_xTc, s + 1)
                hold(dve, s_state, s)
                dve.tensor_tensor(xdec[:, :, :].rearrange("p b (e n) -> p b e n", n=SP_),
                                  xn[:, :, :].rearrange("p b (e n) -> p b e n", n=SP_),
                                  cols[:, 1, :, bass.ds(s * 2, 2)][:, :, :, None].broadcast_to([P, NB, 2, SP_]),
                                  ALU.mult).then_inc(s_xdec, 1)
                st = state.rearrange("p (b n) -> p b n", n=SN)
                pd = prod.rearrange("p (b n) -> p b n", n=SN)
                dve.wait_ge(s_st, s * 16 + 16)
                o.last(dve.tensor_tensor(st, st, dsmp[:, :, None].broadcast_to([P, TS, SN]), ALU.mult))
                o.step(dve.tensor_tensor(pd, rows[:, 0, :].rearrange("p (b n) -> p b n", n=SN),
                                         xsmp[:, :, None].broadcast_to([P, TS, SN]), ALU.mult))
                dve.wait_ge(s_den, s + 1)
                o.step(dve.tensor_reduce(rden, pov[:, 192:256].rearrange("p (k n) -> p n k", n=16), AX_X, ALU.add))
                o.step(dve.tensor_tensor(rden, rden, s5[:, PAGES, :], ALU.add))
                o.step(dve.reciprocal(rden, rden))
                second = rden.rearrange("p (n m) -> p n m", m=2)[:, :, 1]
                o.step(dve.tensor_scalar(second, second, lam[:, 1:2], None, ALU.mult))
                o.step(dve.tensor_tensor(s5, s5, rden[:, None, :].broadcast_to([P, PAGES + 1, 16]), ALU.mult))
                sp = s5.rearrange("p k (n m) -> p k n m", m=2)
                dve.tensor_tensor(a5, sp[:, :, :, 0], sp[:, :, :, 1], ALU.add).then_inc(s_a5, 1)
                dve.wait_ge(s_a5, s + 1)
                o.step(dve.tensor_tensor(onew[:, :], vs[:, :, bass.ds(s, 1)].rearrange("p n b -> p (n b)"),
                                         a5[:, PAGES, :], ALU.mult))
                dve.wait_ge(s_state, s + 1)
                hold(dve, s_hout, 16 * s)
                o.step(dve.tensor_copy(hst[:, 1, :], pov[:, 0:P]))
                for b in range(1, NB):
                    for e in range(2):
                        r = slice(e * SP_, (e + 1) * SP_)
                        m = dve.scalar_tensor_tensor(out=hst[:, b + 1, r], in0=hst[:, b, r],
                                                     scalar=dec[:, e, (b + 1) * P - 1:(b + 1) * P],
                                                     in1=pov[:, b * P + e * SP_:b * P + (e + 1) * SP_],
                                                     op0=ALU.mult, op1=ALU.add)
                        if e == 0:
                            o.last(m)
                        elif b < NB - 1:
                            o.step(m)
                        else:
                            m.then_inc(s_hst, 1)
                dve.tensor_tensor(st, st, pd, ALU.add).then_inc(s_stn, 1)
                dve.wait_ge(s_stn, s + 1)
                o.step(dve.tensor_tensor(pd, st, rows[:, 1, :].rearrange("p (b n) -> p b n", n=SN), ALU.mult))
                o.step(dve.tensor_reduce(ysmp, pd, AX_X, ALU.add))
                dve.wait_ge(s_y, s + 1)
                skip = par[:, bass.ds(s + PARAM_AT["d_skip"][0], 1)]
                o.last(dve.scalar_tensor_tensor(out=yv[:, TP:T], in0=xs[:, TP:T], scalar=skip, in1=ysmp,
                                                op0=ALU.mult, op1=ALU.add))
                o.step(dve.scalar_tensor_tensor(out=yv[:, 0:TP], in0=xs[:, 0:TP], scalar=skip, in1=ptr[:, :],
                                                op0=ALU.mult, op1=ALU.add))
                dve.tensor_tensor(mix[:, bass.ds(s + AH, 1), :].rearrange("p a t -> p (a t)"), yv, zg,
                                  ALU.mult).then_inc(s_ymix, 1)
            if proj:
                dve.wait_ge(s_read[0], read_no("zx", i, 0))
                if ssd:
                    dve.wait_ge(s_ymix, s + 1)
                convolve(o, dve, i, xs)
            if ssd:
                dve.wait_ge(s_oT, s + 1)
                dve.tensor_tensor(o64[:, :, bass.ds(s, 1)].rearrange("p n b -> p (n b)"), onew[:, :],
                                  pov[:, 256:256 + 63 + 1:AH + 1], ALU.add).then_inc(s_o64, 1)

        def pages_pool(pool, s):
            for w, name in enumerate(("cache_k", "cache_v")):
                if w:
                    hold_alone(pool, s_ymix, s, s_beat)
                    hold_alone(pool, s_stout, s * 16, s_beat)
                    pool.dma_start(state.rearrange("p (b n) -> p b n", n=SN),
                                   a["state_ssm"][:, bass.ds(s, 1)].rearrange("b a q n -> q b (a n)")
                                   ).then_inc(s_st, 16)
                for k in range(PAGES):
                    if w == 0:
                        hold_alone(pool, s_opv, s, s_beat)
                    else:
                        hold_alone(pool, s_prod, s * 4 + k + 1, s_beat)
                    page = pool.value_load(table[0:1, bass.ds(s * PAGES + k, 1)], min_val=0, max_val=a[name].shape[0] - 1)
                    pool.dma_start(kv[:, k, :], a[name][bass.ds(page, 1)].rearrange("a p n -> p (a n)")
                                   ).then_inc(s_page[k], 16)
            hold_alone(pool, s_stn, s + 1, s_beat)
            pool.dma_start(a["ssm_s"][:, bass.ds(s, 1)].rearrange("b a q n -> q b (a n)"),
                           state.rearrange("p (b n) -> p b n", n=SN)).then_inc(s_stout, 16)
            hold_alone(pool, s_hst, s + 1, s_beat)
            pool.dma_start(a["ssm_p"][bass.ds(s, 1)].rearrange("a p n -> p (a n)"), hst[:, NB, :]).then_inc(s_hout, 16)

        oq = prod[:, 0:AH * TS]
        orr = prod[:, 128:128 + AH * TS]
        yq = gap[:, :, :].rearrange("p a b -> p (a b)")[:, 0:T]
        yr = cdec[:, :, :].rearrange("p a b -> p (a b)")[:, 0:T]
        yr2 = dec[:, :, :].rearrange("p a b -> p (a b)")[:, 0:T]
        of = o64[:, :, :].rearrange("p n b -> p (n b)")

        def ends_act(act):
            act.wait_ge(s_o64, TS)
            act.activation(oq, of, ACT.Square).then_inc(s_osn_a, 1)
            for c in range(SH // 2):
                hold(act, s_ysum, c - 1)
                act.activation((yq, yv)[c % 2], mix[:, AH + c, :], ACT.Square).then_inc(s_ysq, 1)
            act.wait_ge(s_osn, 1)
            act.activation(orr, orr, ACT.Sqrt).then_inc(s_osn_a, 1)
            act.wait_ge(s_yvar, 1)
            act.activation(yr, yr, ACT.Sqrt).then_inc(s_yroot, 1)

        def ends_pe(pe):
            pe.wait_ge(s_osn_a, 1)
            pe.matmul(pov[:, 0:AH * TS], ones, oq, start=True, stop=True).then_inc(s_osn_p, 1)
            for c in range(SH // 2):
                pe.wait_ge(s_ysq, c + 1)
                for b in range(2):
                    m = pe.matmul(pst[:, b, 0:HT], ones, (yq, yv)[c % 2][:, b * HT:(b + 1) * HT], start=(c == 0),
                                  stop=(c == SH // 2 - 1))
                m.then_inc(s_ysum, 1)

        def ends_dve(dve, o):
            dve.wait_ge(s_osn_p, 1)
            dve.tensor_scalar(orr, pov[:, 0:AH * TS], 1.0 / P, EPS, ALU.mult, ALU.add).then_inc(s_osn, 1)
            dve.wait_ge(s_osn_a, 2)
            o.step(dve.reciprocal(orr, orr))
            dve.scalar_tensor_tensor(out=mix[:, 0:AH, TP:T].rearrange("p n b -> p n b"), in0=o64[:, :, :],
                                     scalar=sub8[:, 0:1], in1=orr.rearrange("p (n b) -> p n b", b=TS),
                                     op0=ALU.mult, op1=ALU.mult).then_inc(s_mixed_all, 1)
            dve.wait_ge(s_ysum, SH // 2)
            dve.tensor_scalar(halves(yr), pst[:, :, 0:HT], 1.0 / SI, EPS, ALU.mult, ALU.add).then_inc(s_yvar, 1)
            dve.wait_ge(s_yroot, 1)
            o.step(dve.reciprocal(yr2, yr))
            for c in range(SH // 2):
                dve.scalar_tensor_tensor(out=mix[:, AH + c, :], in0=mix[:, AH + c, :], scalar=pr("ssm_norm", c),
                                         in1=yr2, op0=ALU.mult, op1=ALU.mult).then_inc(s_mixed_all, 1)

        scratch = 2 * T + 2 * T
        memh, at = carve(scratch, DC, NM)
        kvx, at = carve(at, 2, NM)
        qx, at = carve(at, T)
        knx, at = carve(at, NM)
        qnx, at = carve(at, T)
        ksx, at = carve(at, NM)
        qsx, at = carve(at, T)
        krx, at = carve(at, NM)
        qrx, at = carve(at, T)
        px, at = carve(at, NB, NM)
        pTx, at = carve(at, 2, TP)
        vnx, at = carve(at, 2, P)
        qsn, at = carve(at, XD)
        qdx, at = carve(at, TS * XD)
        qbx, at = carve(at, TS * XD)
        sx, at = carve(at, TS, 2)
        smx, at = carve(at, 64)
        assert at <= ARENA, at
        mixf = mix[:, :, :].rearrange("p a b -> p (a b)")
        kcx, at = carve(4 * T, TS * 2, XD, of=mixf)
        vcx, at = carve(at, TS * 2, XD, of=mixf)
        prx, at = carve(at, TS * 2, XD, of=mixf)
        assert at <= DC * T
        nmx, dsx = smx[:, 0:NB], smx[:, NB:2 * NB]
        mxs, mxc, mxd, rsx = smx[:, 8:16], smx[:, 16:17], smx[:, 24:32], smx[:, 32:40]

        s_xin = sem("s_xin")
        s_memin = sem("s_memin")
        s_xv = sem("s_xv")
        s_xroot = sem("s_xroot")
        s_xvTc = sem("s_xvTc")
        s_xexp = sem("s_xexp")
        s_xpTc = sem("s_xpTc")
        s_xoc = sem("s_xoc")
        s_xqbc = sem("s_xqbc")
        s_xkc = sem("s_xkc")
        s_xvc = sem("s_xvc")
        s_xse = sem("s_xse")
        s_xout = sem("s_xout")

        DVE_STEPS = ("var", "kn", "qn", "max", "qd", "p", "m", "md", "sh", "ps", "soc")
        PE_STEPS = ("sum", "vT", "sc", "pT0", "pT1", "qb", "o", "mT", "mb", "den", "so")
        s_xdve = sem("s_xdve")
        s_xpe = sem("s_xpe")

        def at_dve(step, heads):
            return (heads - 1) * len(DVE_STEPS) + (DVE_STEPS.index(step) + 1)

        def at_pe(step, heads):
            return (heads - 1) * len(PE_STEPS) + (PE_STEPS.index(step) + 1)

        def out_pe(pe, i, first=False, last=False):
            for j in range(4):
                pb = j % 2
                ready_tile(pe, "out", i, j, pb)
                project(pe, PLACES["out"][4][j], pb, mix, 0, DC, after=(s_mixed_all, 2 - AH) if first and j == 0 else None)
                if last and j == 0:
                    norm_pe(pe, 1, nrstd, NM)

        def out_dve(dve, o, i, last=False):
            for j in range(4):
                pb = j % 2
                hold_alone(dve, s_tile, tile_no("out", i, j) + 1, s_beat)
                add_chunk(dve, o, i * 4 + j, pb)
                if last and j == 0:
                    norm_dve(dve, o, 1, memh, memh, "norm_mem", NM)

        def memory_squares(dve, o):
            dve.wait_ge(s_memin, 16)
            for c in range(DC):
                dst = nrt if c else nrstd
                o.step(dve.tensor_tensor(dst[:, 0:NM], memh[:, c, :], memh[:, c, :], ALU.mult))
                if c:
                    o.step(dve.tensor_tensor(nrstd[:, 0:NM], nrstd[:, 0:NM], nrt[:, 0:NM], ALU.add))
            dve.sem_inc(s_sq, 1)

        def cross_pe(pe, c, proj, att):
            def quarters(j, n0, n1):
                if proj:
                    slot, pb = PLACES["mem"][4][j], PLACES["mem"][5][j]
                    if n0 == 0:
                        ready_tile(pe, "mem", c, j, pb)
                    project(pe, slot, pb, h if j == 2 else memh, 4 * n0, 4 * n1, T if j == 2 else NM,
                            after=(s_h, 2 * DC + 1) if j == 2 and not att else None)

            quarters(0, 0, 2)
            if att:
                pe.wait_ge(s_xv, c)
                hold(pe, s_xdve, at_dve("soc", c - 1))
                pe.matmul(ptr[:, 0:NM], ones, ksx, start=True, stop=True)
                for b in range(2):
                    m = pe.matmul(pst[:, b, 0:HT], ones, qsx[:, b * HT:(b + 1) * HT], start=True, stop=True)
                m.then_inc(s_xpe, 1)
            quarters(0, 2, 4)
            if not att:
                norm_pe(pe, 2, nsum, T)
            quarters(1, 0, 2)
            if att:
                for b in range(2):
                    pe.transpose(pov[:, b * P:(b + 1) * P], kvx[:, 1, b * P:(b + 1) * P], ident)
                pe.wait_ge(s_xdve, at_dve("qn", c))
                pe.transpose(pov[0:TS, 256:256 + P], qnx[:, TP:T], ident).then_inc(s_xpe, 1)
                for b in range(NB):
                    m = pe.matmul(pst[:, b // 2, (b % 2) * NM:(b % 2 + 1) * NM], qnx[:, b * P:(b + 1) * P], knx,
                                  start=True, stop=True)
                m.then_inc(s_xpe, 1)
            quarters(1, 2, 4)
            quarters(2, 0, 1)
            if att:
                pe.wait_ge(s_xdve, at_dve("p", c))
                for k in range(2):
                    if k:
                        pe.wait_ge(s_xpTc, (c - 1) * 2 + 1)
                        quarters(2, 1, 2)
                    for b in range(NB):
                        m = pe.transpose(ptr[:, b * P:(b + 1) * P], px[:, b, k * P:(k + 1) * P], ident)
                    m.then_inc(s_xpe, 1)
                pe.wait_ge(s_xdve, at_dve("qd", c))
                for b in range(2):
                    m = pe.matmul(pst[:, b, :], ones[0:TS, :], qdx[0:TS, b * 512:(b + 1) * 512], start=True, stop=True)
                m.then_inc(s_xpe, 1)
                quarters(2, 2, 3)
                pe.wait_ge(s_xpTc, c * 2)
                for k in range(2):
                    m = pe.matmul(pov[:, :], vnx[:, k, :], pTx[:, k, :], start=(k == 0), stop=(k == 1))
                m.then_inc(s_xpe, 1)
            else:
                quarters(2, 1, 3)
            quarters(2, 3, 4)
            if att:
                pe.wait_ge(s_xdve, at_dve("m", c))
                pe.transpose(ptr[0:TS, 0:P], mxs, ident).then_inc(s_xpe, 1)
                pe.wait_ge(s_xdve, at_dve("md", c))
                pe.matmul(ptr[:, P:P + TS], ones[0:TS, :], mxd[0:TS, :], start=True, stop=True).then_inc(s_xpe, 1)
                pe.wait_ge(s_xse, c)
                pe.matmul(ptr[:, 256:256 + 2 * TS], ones, sx[:, :, :].rearrange("p a b -> p (a b)"),
                          start=True, stop=True).then_inc(s_xpe, 1)
                pe.wait_ge(s_xdve, at_dve("ps", c))
                pe.wait_ge(s_xoc, c)
                pe.wait_ge(s_xvc, c * 16)
                for t in range(TS):
                    for k in range(2):
                        m = pe.matmul(pov[:, t:t + 1], vcx[:, 2 * t + k, :], sx[:, t, k:k + 1],
                                      start=(k == 0), stop=(k == 1))
                m.then_inc(s_xpe, 1)

        def cross_act(act, o, c, proj, att):
            if att:
                act.wait_ge(s_xdve, at_dve("var", c))
                o.last(act.activation(krx, krx, ACT.Sqrt))
                act.activation(qrx, qrx, ACT.Sqrt).then_inc(s_xroot, 1)
                act.wait_ge(s_xpe, at_pe("vT", c))
                hold(act, s_xpe, at_pe("o", c - 1))
                hold(act, s_xdve, at_dve("qd", c - 1))
                o.last(act.activation(vnx[:, :, :].rearrange("p a b -> p (a b)"), pov[:, 0:NM], ACT.Copy))
                act.activation(qsn[0:TS, :], pov[0:TS, 256:256 + P], ACT.Copy).then_inc(s_xvTc, 1)
                act.wait_ge(s_xdve, at_dve("max", c))
                hold(act, s_xpe, at_pe("pT1", c - 1))
                for b in range(NB):
                    m = act.activation(px[:, b, :], pst[:, b // 2, (b % 2) * NM:(b % 2 + 1) * NM], ACT.Exp,
                                       bias=nmx[:, b:b + 1], scale=X_SCALE, accum_out=dsx[:, b:b + 1])
                    o.last(m) if b < NB - 1 else m.then_inc(s_xexp, 1)
            if proj:
                for j in range(2):
                    act.wait_ge(s_tile, tile_no("mem", c, j) + 1)
                    hold(act, s_xdve, at_dve("kn", c)) if j == 0 else None
                    hold(act, s_xout, 32 * c)
                    o.tell(act.activation(kvx[:, j, :], pj[:, j, 0, 0:NM], ACT.Copy), s_read[j],
                             read_no("mem", c, j))
                hold(act, s_xpe, at_pe("sum", c))
                o.last(act.activation(ksx, kvx[:, 0, :], ACT.Square))
            if att:
                for k in range(2):
                    act.wait_ge(s_xpe, at_pe(("pT0", "pT1")[k], c))
                    act.activation(pTx[:, k, :], ptr[:, :], ACT.Copy).then_inc(s_xpTc, 1)
                act.wait_ge(s_xpe, at_pe("qb", c))
                hold(act, s_xdve, at_dve("m", c - 1))
                act.activation(qbx, pst[:, :, :].rearrange("p a b -> p (a b)"), ACT.Copy).then_inc(s_xqbc, 1)
            if att:
                act.wait_ge(s_xpe, at_pe("o", c))
                act.activation(mix[:, bass.ds(c - 1, 1), 0:TP].rearrange("p a t -> p (a t)"), pov[:, :],
                               ACT.Copy).then_inc(s_xoc, 1)
                act.wait_ge(s_xdve, at_dve("sh", c))
                act.activation(sx[:, :, :].rearrange("p a b -> p (a b)"), sx[:, :, :].rearrange("p a b -> p (a b)"),
                               ACT.Exp, scale=X_SCALE).then_inc(s_xse, 1)
            if proj:
                act.wait_ge(s_tile, tile_no("mem", c, 2) + 1)
                hold(act, s_xdve, at_dve("qn", c))
                o.tell(act.activation(halves(qx), pair(0), ACT.Copy), s_read[0], read_no("mem", c, 2))
                act.activation(qsx, qx, ACT.Square).then_inc(s_xv, 1)

        def cross_dve(dve, o, c):
            a0 = c - 1
            dve.wait_ge(s_xpe, at_pe("sum", c))
            o.last(dve.tensor_scalar(krx, ptr[:, 0:NM], 1.0 / P, EPS, ALU.mult, ALU.add))
            dve.tensor_scalar(halves(qrx), pst[:, :, 0:HT], 1.0 / P, EPS, ALU.mult, ALU.add).then_inc(s_xdve, 1)
            dve.wait_ge(s_xroot, c)
            o.last(dve.reciprocal(krx, krx))
            o.step(dve.reciprocal(qrx, qrx))
            hold(dve, s_xout, 32 * a0)
            dve.scalar_tensor_tensor(out=knx, in0=kvx[:, 0, :], scalar=pr("kx_norm"), in1=krx, op0=ALU.mult,
                                     op1=ALU.mult).then_inc(s_xdve, 1)
            dve.scalar_tensor_tensor(out=qnx, in0=qx, scalar=pr("qx_norm"), in1=qrx, op0=ALU.mult,
                                     op1=ALU.mult).then_inc(s_xdve, 1)
            dve.wait_ge(s_xpe, at_pe("sc", c))
            sc = pst[:, :, :].rearrange("p a (b k) -> p (a b) k", k=NM)
            o.step(dve.tensor_reduce(nmx, sc, AX_X, ALU.max))
            dve.tensor_scalar(nmx, nmx, -X_SCALE, None, ALU.mult).then_inc(s_xdve, 1)
            dve.wait_ge(s_xvTc, c)
            hold(dve, s_xpe, at_pe("qb", a0))
            dve.tensor_tensor(qdx[0:TS].rearrange("p (b n) -> p b n", n=XD),
                              qsn[0:TS][:, None, :].broadcast_to([TS, TS, XD]),
                              ident[0:TS, 0:TS][:, :, None].broadcast_to([TS, TS, XD]), ALU.mult).then_inc(s_xdve, 1)
            dve.wait_ge(s_xexp, c)
            o.step(dve.reciprocal(dsx, dsx))
            dve.tensor_tensor(px[:, :, :], px[:, :, :], dsx[:, :, None].broadcast_to([P, NB, NM]),
                              ALU.mult).then_inc(s_xdve, 1)
            dve.wait_ge(s_xqbc, c)
            dve.wait_ge(s_xkc, c * 16)
            hold(dve, s_xpe, at_pe("so", a0))
            qv = qbx.rearrange("p (b n) -> p b n", n=XD)[:, :, None, :].broadcast_to([P, TS, 2, XD])
            o.step(dve.tensor_tensor(prx[:, :, :].rearrange("p (b k) n -> p b k n", k=2),
                                     kcx[:, :, :].rearrange("p (b k) n -> p b k n", k=2), qv, ALU.mult))
            o.step(dve.tensor_reduce(sx[:, :, :].rearrange("p a b -> p (a b)"), prx[:, :, :], AX_X, ALU.add))
            dve.tensor_reduce(mxs, sx[:, :, :], AX_X, ALU.max).then_inc(s_xdve, 1)
            dve.wait_ge(s_xpe, at_pe("mT", c))
            o.step(dve.tensor_reduce(mxc[0:TS], ptr[0:TS, 0:P], AX_X, ALU.max))
            dve.tensor_scalar(mxd[0:TS], ident[0:TS, 0:TS], mxc[0:TS], None, ALU.mult).then_inc(s_xdve, 1)
            dve.wait_ge(s_xpe, at_pe("mb", c))
            dve.tensor_tensor(sx[:, :, :], sx[:, :, :], ptr[:, P:P + TS][:, :, None].broadcast_to([P, TS, 2]),
                              ALU.subtract).then_inc(s_xdve, 1)
            dve.wait_ge(s_xpe, at_pe("den", c))
            o.step(dve.tensor_reduce(rsx, ptr[:, 256:256 + 2 * TS].rearrange("p (a b) -> p a b", b=2), AX_X, ALU.add))
            o.step(dve.reciprocal(rsx, rsx))
            dve.tensor_tensor(sx[:, :, :], sx[:, :, :], rsx[:, :, None].broadcast_to([P, TS, 2]),
                              ALU.mult).then_inc(s_xdve, 1)
            dve.wait_ge(s_xpe, at_pe("so", c))
            dve.tensor_scalar(mix[:, bass.ds(a0, 1), TP:T].rearrange("p a t -> p (a t)"), pov[:, 0:TS], 0.0, None,
                              ALU.add).then_inc(s_xdve, 1)

        def cross_pool(pool, c):
            hold_alone(pool, s_xdve, at_dve("m", c), s_beat)
            pool.dma_start(kcx[:, :, :], a["mem_k"][bass.ds(c, 1)].rearrange("a (k p) d -> p (a k) d", p=P)
                           ).then_inc(s_xkc, 16)
            hold_alone(pool, s_xpe, at_pe("so", c), s_beat)
            pool.dma_start(vcx[:, :, :], a["mem_v"][bass.ds(c, 1)].rearrange("a (k p) d -> p (a k) d", p=P)
                           ).then_inc(s_xvc, 16)
            hold_alone(pool, s_xdve, at_dve("kn", c + 1), s_beat)
            pool.dma_start(a["mk_out"][bass.ds(c, 1)].rearrange("a p t -> p (a t)"), knx).then_inc(s_xout, 16)
            pool.dma_start(a["mv_out"][bass.ds(c, 1)].rearrange("a p t -> p (a t)"), kvx[:, 1, :]).then_inc(s_xout, 16)

        def wo_pe(pe):
            tile0, loads, uses, _, slots, _ = PLACES["wo"]
            pe.wait_ge(s_xoc, XH)
            pe.wait_ge(s_xdve, at_dve("soc", XH))
            for n in range(DC):
                slot, pb = slots[n // 4], n % 2
                if n % 4 == 0:
                    pe.wait_ge(s_loaded[slot], 16 * (loads[slot] + 1))
                pe.wait_ge(s_read[pb], uses[pb] + n // 2)
                for c in range(XH):
                    w = ring[:, slot, ((n % 4) * XH + c) * P:((n % 4) * XH + c + 1) * P]
                    for b in range(2):
                        m = pe.matmul(pj[:, pb, b, 0:HT], w, mix[:, c, b * HT:(b + 1) * HT],
                                      start=(c == 0), stop=(c == XH - 1))
                m.then_inc(s_wo, 1)

        def wo_dve(dve, o):
            o.step(dve.memset(nsum, 0.0))
            for n in range(DC):
                dve.wait_ge(s_wo, n + 1)
                dve.sem_inc(s_beat, 1)
                add_chunk(dve, o, n, n % 2)
            dve.sem_inc(s_sq, 1)

        s_wo = sem("s_wo")

        BL = NB + 1
        pks, at = carve(0, PH, PK)
        pq, at = carve(at, 2, T)
        kb, at = carve(at, 2, PK)
        assert at <= 2 * T + 2 * T + DC * NM, at
        big = at = 4800
        near, at = carve(at, 2, PK)
        near8, at = carve(at, 2, PK)
        hit, at = carve(at, 2, PK)
        top, at = carve(at, 2, TOPK)
        cand, at = carve(at, 2, TOPK * TOPK)
        ftop, at = carve(at, TOPK)
        ints, at = carve(at, 5, TOPK)
        ints = ints.bitcast(U32)
        topi, fpos, fhi, flo = ints[:, 0:2, :], ints[:, 2, :], ints[:, 3, :], ints[:, 4, :]
        sid, at = carve(at, BL, PH, 2 * TOPK)
        fsum, at = carve(at, BL, PH, TOPK)
        fa, at = carve(at, BL, PH, TOPK)
        fb, at = carve(at, BL, PH, TOPK)
        gw, at = carve(at, BL, PH, TOPK)
        eidf, at = carve(at, P)
        cols8, at = carve(at, 2, DC, TS)
        later, at2 = carve(at, PH, 2, (NB - 1) * PK)
        hsn, at = carve(at, D)
        xsn, at = carve(at, D)
        pick8, at = carve(at, TS, P)
        at = max(at, at2)
        eidi = arena[:, at:at + BL * P].bitcast(I32).rearrange("p (a b) -> p a b", b=P)
        assert at + BL * P <= ARENA, at + BL * P
        one, at2 = carve(0, P, TOPK)
        tb, at2 = carve(at2, D)
        acol, at2 = carve(at2, 16)
        adot, at2 = carve(at2, P)
        wexp, at2 = carve(at2, P)
        gtmp, at2 = carve(at2, 2, PH)
        sel, at2 = carve(at2, 2, P)
        act8, at2 = carve(at2, TS)
        w8, at2 = carve(at2, TS)
        g8, at2 = carve(at2, TS)
        wm, at2 = carve(at2, TS, TS)
        assert at2 <= big, (at2, big)
        eid8 = sb("eid8", [P, TS], I32)
        ixs = sb("ixs", [P, 8], I32)
        junk = one.rearrange("p a b -> p (a b)")
        hnat = mixf[:, 0:NB * D].rearrange("p (b d) -> p b d", d=D)
        hf = h[:, :, :].rearrange("p a b -> p (a b)")
        acc = hf[:, 0:NB * D].rearrange("p (b d) -> p b d", d=D)
        ringf = ring[:, :, :]
        xf = x[:, :, :].rearrange("p a b -> p (a b)")

        def row(s):
            return ringf[:, s, :] if s < 4 else xf[:, (s - 4) * D:(s - 3) * D]

        pjf = pj[:, :, :, :].rearrange("p a b n -> p (a b n)")

        s_keys = sem("s_keys")
        s_pq = sem("s_pq")
        s_psc = sem("s_psc")
        s_top = sem("s_top")
        s_turn = sem("s_turn")
        s_turnc = sem("s_turnc")
        s_oh = sem("s_oh")
        s_ge = sem("s_ge")
        s_eid = sem("s_eid")
        s_ix = sem("s_ix")
        s_got = [sem(f"s_got{k}") for k in range(8)]
        s_used = sem("s_used")
        s_dot = sem("s_dot")
        s_gelu = sem("s_gelu")
        s_tb = sem("s_tb")
        s_blk = sem("s_blk")
        s_e8 = sem("s_e8")
        s_e8c = sem("s_e8c")
        s_hm = sem("s_hm")
        s_hb = sem("s_hb")
        s_w8 = sem("s_w8")
        s_fin = sem("s_fin")

        def score_of(b, c):
            return pst[:, c, b * PK:(b + 1) * PK] if b < NB else (ptr, pov)[c][0:TS, 0:PK]

        def heads_pe(pe, i, first, proj=True):
            for e in range(2):
                if proj:
                    ready_tile(pe, "peer", i, e, e)
                    project(pe, e, e, h, 0, 8, after=(s_h, 3 * DC + 1) if first and e == 0 else None)
                if not (first and e == 0):
                    hd = i * 2 + e - 1
                    o = 1 - e
                    pe.wait_ge(s_pq, hd + 1)
                    hold(pe, s_top, hd)
                    for b in range(BL):
                        for c in range(2):
                            r = slice(c * AD, (c + 1) * AD)
                            dst = score_of(b, c)
                            m = pe.matmul(dst, pq[r, o, b * P:min((b + 1) * P, T)], kb[r, o, :],
                                          start=True, stop=True)
                    m.then_inc(s_psc, 1)
                if proj:
                    project(pe, e, e, h, 8, DC, after=(s_h, 3 * DC + 1) if first and e == 0 else None)
                else:
                    break

        def heads_act(act, o, i):
            for e in range(2):
                act.wait_ge(s_tile, tile_no("peer", i, e) + 1)
                hold(act, s_psc, i * 2 + e - 1)
                o.last(act.activation(kb[:, e, :], pks[:, bass.ds(i * 2 + e, 1), :].rearrange("p a n -> p (a n)"),
                                      ACT.Copy))
                act.activation(halves(pq[:, e, :]), pair(e), ACT.Copy).then_inc(s_read[e], 1)
                act.wait_ge(s_read[e], read_no("peer", i, e))
                act.sem_inc(s_pq, 1)

        def best_keys(dve, o, n, src, b, hd):
            r = slice(0, n)
            o.last(dve.max(top[r, 0, 0:8], src[r, 0, :]))
            o.step(dve.max(top[r, 1, 0:8], src[r, 1, :]))
            for c in range(2):
                o.last(dve.match_replace(hit[r, c, :], top[r, c, 0:8], src[r, c, :], NEG))
            o.last(dve.max_index(topi[r, 0, 0:8], top[r, 0, 0:8], src[r, 0, :]))
            o.step(dve.max_index(topi[r, 1, 0:8], top[r, 1, 0:8], src[r, 1, :]))
            o.last(dve.max(top[r, 0, 8:16], hit[r, 0, :]))
            o.step(dve.max(top[r, 1, 8:16], hit[r, 1, :]))
            o.last(dve.max_index(topi[r, 0, 8:16], top[r, 0, 8:16], hit[r, 0, :]))
            o.last(dve.max_index(topi[r, 1, 8:16], top[r, 1, 8:16], hit[r, 1, :]))
            o.step(dve.tensor_tensor(cand[r, 0, :].rearrange("p (a b) -> p a b", b=TOPK),
                                     top[r, 0, :][:, :, None].broadcast_to([n, TOPK, TOPK]),
                                     top[r, 1, :][:, None, :].broadcast_to([n, TOPK, TOPK]), ALU.add))
            o.step(dve.max(ftop[r, 0:8], cand[r, 0, :]))
            o.last(dve.match_replace(cand[r, 1, :], ftop[r, 0:8], cand[r, 0, :], NEG))
            o.step(dve.max_index(fpos[r, 0:8], ftop[r, 0:8], cand[r, 0, :]))
            o.step(dve.max(ftop[r, 8:16], cand[r, 1, :]))
            o.step(dve.max_index(fpos[r, 8:16], ftop[r, 8:16], cand[r, 1, :]))
            o.last(dve.tensor_scalar(fhi[r], fpos[r], 4, None, ALU.logical_shift_right))
            o.step(dve.tensor_scalar(flo[r], fpos[r], TOPK - 1, None, ALU.bitwise_and))
            kept = lambda v: v[r, bass.ds(b, 1), bass.ds(hd, 1), :].rearrange("p b a k -> p (b a k)")
            o.last(dve.tensor_scalar(kept(fsum), ftop[r], 0.0, None, ALU.add))
            o.last(dve.tensor_scalar(kept(fa), fhi[r], 0.0, None, ALU.add))
            o.last(dve.tensor_scalar(kept(fb), flo[r], 0.0, None, ALU.add))
            o.step(dve.tensor_scalar(kept(sid), topi[r].rearrange("p c k -> p (c k)"), 0.0, None, ALU.add))

        def heads_dve(dve, o, hd, samples=True):
            hold_alone(dve, s_psc, hd + 1, s_beat)
            o.last(dve.tensor_copy(later[:, bass.ds(hd, 1), :, :].rearrange("p a c n -> p (a c) n"),
                                   pst[:, :, P:TP]))
            o.last(dve.tensor_copy(near, pst[:, :, 0:P]))
            o.last(dve.tensor_copy(near8[0:TS, 0, :], ptr[0:TS, 0:PK]))
            o.step(dve.tensor_copy(near8[0:TS, 1, :], pov[0:TS, 0:PK]))
            dve.sem_inc(s_top, 1)
            best_keys(dve, o, P, near, 0, hd)
            if samples:
                best_keys(dve, o, TS, near8, NB, hd)

        def turn_half(pe, src, n):
            hold(pe, s_turnc, n - 1)
            for c in range(DC // 2):
                v = src(n % 2 * (DC // 2) + c)
                w = v.shape[1]
                k = n % 2 * (DC // 2) + c
                m = pe.transpose(pjf[0:w, k * P:(k + 1) * P], v, ident)
            m.then_inc(s_turn, 1)

        def turn_pe(pe):
            pe.wait_ge(s_read[0], uses_of("peer", 0))
            pe.wait_ge(s_read[1], uses_of("peer", 1))
            for n in range(4 * NB):
                v, b = (h, x)[n // (2 * NB)], n // 2 % NB
                turn_half(pe, lambda c: v[:, c, b * P:(b + 1) * P], n)

        def turn_act(act):
            act.wait_ge(s_top, PH)
            act.activation(cols8[:, 0, :, :], h[:, :, TP:T], ACT.Copy)
            act.activation(cols8[:, 1, :, :], x[:, :, TP:T], ACT.Copy)
            for n in range(4 * NB):
                v, b, half = (hnat, acc)[n // (2 * NB)], n // 2 % NB, slice(n % 2 * (D // 2), (n % 2 + 1) * (D // 2))
                act.wait_ge(s_turn, n + 1)
                act.activation(v[:, b, half], pjf[:, half], ACT.Copy).then_inc(s_turnc, 1)
                if n == 1:
                    act.wait_ge(s_turnc, 2)
                    act.activation(tb, hnat[:, 0, :], ACT.Copy).then_inc(s_tb, 1)

        def samples_turn_pe(pe):
            pe.wait_ge(s_turnc, 4 * NB)
            for n in range(4 * NB, 4 * NB + 4):
                turn_half(pe, lambda c: cols8[:, (n - 4 * NB) // 2, c, :], n)

        def samples_turn_act(act):
            for n in range(4 * NB, 4 * NB + 4):
                v, half = (hsn, xsn)[(n - 4 * NB) // 2], slice(n % 2 * (D // 2), (n % 2 + 1) * (D // 2))
                act.wait_ge(s_turn, n + 1)
                act.activation(v[0:TS, half], pjf[0:TS, half], ACT.Copy).then_inc(s_turnc, 1)

        def pick_dve(dve, o, b):
            blk = lambda v: v[:, bass.ds(b, 1), :, :].rearrange("p a h k -> p (a h) k")
            fs, g = blk(fsum), blk(gw)
            dve.tensor_tensor(g, fs, fs[:, :, 0:1].broadcast_to([P, PH, TOPK]), ALU.subtract).then_inc(s_oh, 1)
            one4 = one.rearrange("p (h k) n -> p h k n", k=TOPK)
            for c, f in enumerate((fa, fb)):
                o.step(dve.tensor_tensor(one, f[:, bass.ds(b, 1), :, :].rearrange("p a h k -> p (a h k)")[:, :, None]
                                         .broadcast_to([P, P, TOPK]),
                                         co("iota")[:, None, :].broadcast_to([P, P, TOPK]), ALU.is_equal))
                si = sid[:, bass.ds(b, 1), :, c * TOPK:(c + 1) * TOPK].rearrange("p a h k -> p (a h) k")
                o.step(dve.tensor_tensor(one4, one4, si[:, :, None, :].broadcast_to([P, PH, TOPK, TOPK]), ALU.mult))
                o.step(dve.tensor_reduce(sel[:, c, :], one, AX_X, ALU.add))
            o.last(dve.scalar_tensor_tensor(out=eidf, in0=sel[:, 0, :], scalar=float(PK), in1=sel[:, 1, :],
                                            op0=ALU.mult, op1=ALU.add))
            dve.scalar_tensor_tensor(out=eidi[:, bass.ds(b, 1), :].rearrange("p a n -> p (a n)"), in0=sel[:, 0, :],
                                     scalar=float(PK), in1=sel[:, 1, :], op0=ALU.mult, op1=ALU.add).then_inc(s_eid, 1)
            hold_alone(dve, s_ge, b + 1, s_beat)
            o.step(dve.tensor_reduce(gtmp[:, 0, :], g, AX_X, ALU.add))
            o.step(dve.reciprocal(gtmp[:, 1, :], gtmp[:, 0, :]))
            o.step(dve.tensor_tensor(g, g, gtmp[:, 1, :][:, :, None].broadcast_to([P, PH, TOPK]), ALU.mult))

        def pick_act(act, b):
            act.wait_ge(s_oh, b + 1)
            g = gw[:, bass.ds(b, 1), :, :].rearrange("p a h k -> p (a h) k")
            act.activation(g, g, ACT.Exp).then_inc(s_ge, 1)

        BEFORE8 = NB * 2 * P - P

        def gather(pool, b, i, k, table_rows, base, more=0):
            hold_alone(pool, s_used, i * 8 + (b * 2 * P + base + k + 1 + more), s_beat)
            pool.tensor_copy(ixs[:, k:k + 1],
                             eidi[:, bass.ds(b, 1), bass.ds(i * 8 + k, 1)].rearrange("p a n -> p (a n)")
                             ).then_inc(s_ix, 1)
            pool.wait_ge(s_ix, i * 8 + (b * 2 * P + base + k + 1))
            pool.sem_inc(s_beat, 1)
            pool.indirect_dma_start(out=row(k), out_offset=None, in_=table_rows,
                                    in_offset=bass.IndirectOffsetOnAxis(ap=ixs[:, k:k + 1], axis=0)
                                    ).then_inc(s_got[k], 16)

        def gathers(pool, b, table_rows, base, first=0, more=0):
            with pool.Fori(first, P // 8) as i:
                for k in range(8):
                    gather(pool, b, i, k, table_rows, base, more)

        def experts_pool(pool):
            pool.wait_ge(s_eid, 1)
            for k in range(8):
                if k == RING:
                    pool.wait_ge(s_turnc, 4 * NB)
                gather(pool, 0, 0, k, a["peer_u"], 0)
            gathers(pool, 0, a["peer_u"], 0, 1)
            gathers(pool, 0, a["peer_v"], P)
            with pool.Fori(1, NB - 1) as b:
                hold_alone(pool, s_eid, b + 1, s_beat)
                gathers(pool, b, a["peer_u"], 0)
                gathers(pool, b, a["peer_v"], P)
            pool.wait_ge(s_eid, NB)
            gathers(pool, NB - 1, a["peer_u"], 0)
            pool.wait_ge(s_e8c, 1)
            for w, rows_of in enumerate((a["peer_u"], a["peer_v"])):
                for t in range(TS):
                    pool.wait_ge(s_used, BEFORE8 + w * TS + t + 1)
                    pool.indirect_dma_start(out=row(t), out_offset=None, in_=rows_of,
                                            in_offset=bass.IndirectOffsetOnAxis(ap=eid8[:, t:t + 1], axis=0)
                                            ).then_inc(s_got[t], 16)
            gathers(pool, NB - 1, a["peer_v"], P, more=2 * TS)

        def experts_dve(dve, o, b, more):
            hold_alone(dve, s_tb, b + 1, s_beat)
            o.settle()
            with dve.Fori(0, PH) as i:
                o.enter()
                if more:
                    o.step(dve.tensor_copy(near, later[:, bass.ds(i, 1), :, bass.ds(b * PK, PK)]
                                           .rearrange("p a c n -> p (a c) n")))
                    best_keys(dve, o, P, near, b + 1, i)
                for k in range(16):
                    dve.wait_ge(s_got[k % 8], i * 32 + (k // 8 * 16 + (b * 2 * P + 8) * 2))
                    dve.tensor_tensor_reduce(out=junk, in0=row(k % 8), in1=tb, scale=1.0, scalar=0.0, op0=ALU.mult,
                                             op1=ALU.add, accum_out=acol[:, k:k + 1]).then_inc(s_used, 1)
                    dve.wait_ge(s_used, i * 16 + (b * 2 * P + k + 9))
                o.step(dve.tensor_scalar(adot[:, bass.ds(i * 16, 16)], acol, 0.0, None, ALU.add))
                dve.sem_inc(s_dot, 1)
                o.settle()

        def values_dve(dve, o, b, more=0):
            dve.wait_ge(s_gelu, b + 1)
            o.step(dve.tensor_tensor(wexp, adot, gw[:, bass.ds(b, 1), :, :].rearrange("p a h k -> p (a h k)"),
                                     ALU.mult))
            y = acc[:, bass.ds(b, 1), :].rearrange("p a n -> p (a n)")
            with dve.Fori(0, P // 8) as i:
                for k in range(8):
                    dve.wait_ge(s_got[k], i * 16 + (b * 2 * P + P + 8 + more) * 2)
                    dve.scalar_tensor_tensor(out=y, in0=row(k), scalar=wexp[:, bass.ds(i * 8 + k, 1)], in1=y,
                                             op0=ALU.mult, op1=ALU.add).then_inc(s_used, 1)
                    dve.wait_ge(s_used, i * 8 + (b * 2 * P + P + k + 9 + more))

        def gelu_act(act, b):
            act.wait_ge(s_dot, (b + 1) * PH)
            act.activation(adot, adot, ACT.Gelu).then_inc(s_gelu, 1)

        def experts_act(act, b):
            pick_act(act, b + 1)
            gelu_act(act, b)
            act.activation(tb, hnat[:, bass.ds(b + 1, 1), :].rearrange("p a n -> p (a n)"), ACT.Copy).then_inc(s_tb, 1)

        def half_of(n):
            return slice(n % 2 * (D // 2), (n % 2 + 1) * (D // 2))

        def samples_pe(pe):
            pe.wait_ge(s_blk, 1)
            pe.transpose(ptr[:, 0:TS], eidf[0:TS, :], ident[0:TS, 0:TS])
            pe.transpose(ptr[:, TS:2 * TS], gw[0:TS, NB, :, :].rearrange("p h k -> p (h k)"),
                         ident[0:TS, 0:TS]).then_inc(s_e8, 1)
            pe.wait_ge(s_turnc, 4 * NB + 4)
            for n in range(2 * TS):
                hold(pe, s_hb, n - 1)
                for b in range(n % 2 * 2, n % 2 * 2 + 2):
                    m = pe.matmul(pjf[:, b * 512:(b + 1) * 512], pick8[0:TS, n // 2, :],
                                  hsn[0:TS, b * 512:(b + 1) * 512], start=True, stop=True)
                m.then_inc(s_hm, 1)
            pe.wait_ge(s_hb, 2 * TS)
            pe.wait_ge(s_w8, 1)
            for t in range(TS):
                pe.wait_ge(s_got[t], 16 * (BEFORE8 // 8 + 2))
                for b in range(4):
                    m = pe.matmul(pjf[0:TS, b * 512:(b + 1) * 512], wm[:, t, :], row(t)[:, b * 512:(b + 1) * 512],
                                  start=(t == 0), stop=(t == TS - 1))
                m.then_inc(s_used, 1)

        def samples_act(act, t0, t1):
            for n in range(2 * t0, 2 * t1):
                act.wait_ge(s_hm, n + 1)
                if n // 2 >= NB:
                    act.wait_ge(s_used, BEFORE8 + 8 + n // 2 - NB + 1)
                act.activation(hnat[:, n // 2 % NB, half_of(n)], pjf[:, half_of(n)], ACT.Copy).then_inc(s_hb, 1)

        def samples_known_dve(dve, o):
            o.step(dve.tensor_copy(pick8[0:TS, :, :], ident[0:TS, 0:TS][:, :, None].broadcast_to([TS, TS, P])))
            dve.sem_inc(s_blk, 1)
            dve.wait_ge(s_e8, 1)
            o.step(dve.tensor_copy(g8, ptr[:, TS:2 * TS]))
            dve.tensor_copy(eid8[:, :], ptr[:, 0:TS]).then_inc(s_e8c, 1)

        def samples_dve(dve, o):
            for t in range(TS):
                dve.wait_ge(s_hb, 2 * t + 2)
                dve.wait_ge(s_got[t], 16 * (BEFORE8 // 8 + 1))
                dve.tensor_tensor_reduce(out=junk, in0=row(t), in1=hnat[:, t % NB, :], scale=1.0, scalar=0.0,
                                         op0=ALU.mult, op1=ALU.add, accum_out=act8[:, t:t + 1]).then_inc(s_used, 1)
                dve.wait_ge(s_used, BEFORE8 + t + 9)
            dve.wait_ge(s_gelu, NB + 1)
            o.step(dve.tensor_tensor(w8, w8, g8, ALU.mult))
            dve.tensor_tensor(wm, w8[:, :, None].broadcast_to([P, TS, TS]),
                              co("eye8").rearrange("p (a b) -> p a b", b=TS), ALU.mult).then_inc(s_w8, 1)
            dve.wait_ge(s_used, BEFORE8 + 2 * TS + 8)
            dve.tensor_tensor(xsn[0:TS, :], pjf[0:TS, :], xsn[0:TS, :], ALU.add).then_inc(s_fin, 1)

        block = ctx.enter_context(nc.Block())

        @block.sync
        def _(sp):
            sp.dma_start(par[:, :], a["params"]).then_inc(s_in, 16)
            sp.dma_start(con[:, :], a["consts"]).then_inc(s_in, 16)
            sp.dma_start(wdt[:, :], a["w_dt"].rearrange("p c n -> p (c n)")).then_inc(s_in, 16)
            sp.dma_start(table[:, :], a["pages"]).then_inc(s_in, 16)
            for i in range(4):
                c = slice(i * DC // 4, (i + 1) * DC // 4)
                sp.dma_start(x[:, c, :], a["xT"][:, c, :]).then_inc(s_xpart[i], 16)
            for name, (tile0, loads, uses, runs, slots, pairs) in PLACES.items():
                m = len(slots)
                last = {}
                n = 0
                for nm, _, _, rr, ss, _ in [(k, *v[1:]) for k, v in PLACES.items()]:
                    if nm == name:
                        break
                    for _ in range(rr):
                        for s in ss:
                            last[s] = n
                            n += 1
                for j, s in enumerate(slots):
                    if name == "peer":
                        sp.wait_ge(s_wo, 4 * (s + 1))
                    elif s in last:
                        sp.wait_ge(s_tile, last[s] + 1)
                    sp.dma_start(ring[:, s, :], a["w"][tile0 + j]).then_inc(s_loaded[s], 16)
                if name == "out":
                    sp.wait_ge(s_o64, TS)
                    sp.dma_start(x[:, :, :], a["xT"]).then_inc(s_xin, 16)
                    sp.wait_ge(s_mixed_all, SH // 2 + 1)
                    sp.wait_ge(s_hout, 16 * TS)
                    sp.wait_ge(s_stout, 16 * TS)
                    sp.wait_ge(s_tails, 32)
                    sp.dma_start(memh[:, :, :], a["memT"]).then_inc(s_memin, 16)
                if runs > 1:
                    with sp.Fori(1, runs) as i:
                        for j, s in enumerate(slots):
                            sp.wait_ge(s_tile, i * m + (tile_no(name, 0, j) - m + 1))
                            sp.dma_start(ring[:, s, :],
                                         a["w"][bass.ds(i * m + (tile0 + j), 1)].rearrange("a p n -> p (a n)")
                                         ).then_inc(s_loaded[s], 16)
            for b in range(NB):
                if b == NB - 1:
                    sp.wait_ge(s_fin, 1)
                    sp.dma_start(a["y_s"], xsn[0:TS, :]).then_inc(s_out, 16)
                sp.wait_ge(s_used, (b + 1) * 2 * P + 8 + (2 * TS if b == NB - 1 else 0))
                sp.dma_start(a["y_p"][b], acc[:, b, :]).then_inc(s_out, 16)
            sp.wait_ge(s_out, 16 * (NB + 1))
        @block.gpsimd
        def _(pool):
            with pool.Fori(0, AH) as g:
                attention_stores(pool, g)
            pool.wait_ge(s_kout, 32 * AH)
            pool.wait_ge(s_omix, AH)
            pool.dma_start(prev[:, :, :], a["conv_prev"]).then_inc(s_prev, 16)
            pages_pool(pool, 0)
            with pool.Fori(1, TS) as s:
                pages_pool(pool, s)
            pool.wait_ge(s_conv, CT)
            pool.dma_start(a["conv_s"], tails[:, :, :]).then_inc(s_tails, 16)
            pool.dma_start(a["conv_p"], tailp[:, :, :]).then_inc(s_tails, 16)
            pool.wait_ge(s_tails, 32)
            pool.wait_ge(s_stout, 16 * TS)
            pool.wait_ge(s_hout, 16 * TS)
            pool.wait_ge(s_h, 3 * DC)
            cross_pool(pool, 0)
            with pool.Fori(1, XH) as c:
                cross_pool(pool, c)
            pool.wait_ge(s_xout, 32 * XH)
            pool.wait_ge(s_h, 4 * DC)
            pool.dma_start(pks[:, :, :], a["keys"]).then_inc(s_keys, 16)
            experts_pool(pool)

        @block.tensor
        def _(pe):
            pe.wait_ge(s_in, 16 * N_IN)
            first_norm_pe(pe)
            attention_pe(pe, 0, True, False)
            attention_pe(pe, 1, True, True)
            with pe.Fori(2, AH) as g:
                attention_pe(pe, g, True, True)
            attention_pe(pe, AH, False, True)
            prepare_pe(pe)
            pairs_pe(pe, 0, 0, True, False)
            group_pe(pe, 0)
            pairs_pe(pe, 1, 0, True, True)
            with pe.Fori(2, 5) as i:
                pairs_pe(pe, i, 0, True, True)
            group_pe(pe, 1)
            with pe.Fori(5, 8) as i:
                pairs_pe(pe, i, 1, True, True)
            pairs_pe(pe, 8, 1, False, True)
            ends_pe(pe)
            out_pe(pe, 0, first=True)
            with pe.Fori(1, DC // 4 - 1) as i:
                out_pe(pe, i)
            out_pe(pe, DC // 4 - 1, last=True)
            pe.wait_ge(s_h, 2 * DC)
            cross_pe(pe, 0, True, False)
            cross_pe(pe, 1, True, True)
            with pe.Fori(2, XH) as c:
                cross_pe(pe, c, True, True)
            cross_pe(pe, XH, False, True)
            wo_pe(pe)
            norm_pe(pe, 3, nsum, T)
            heads_pe(pe, 0, True)
            with pe.Fori(1, PH // 2) as i:
                heads_pe(pe, i, False)
            heads_pe(pe, PH // 2, False, proj=False)
            turn_pe(pe)
            pe.wait_ge(s_dot, (NB - 1) * PH)
            samples_turn_pe(pe)
            samples_pe(pe)

        @block.scalar
        def _(act):
            o = Order(act, s_act)
            first_norm_act(act)
            norm_act(act, 0, T)
            act.wait_ge(s_in, 16 * N_IN)
            act.wait_ge(s_dve_lam, 1)
            act.activation(lam[:, 0:2], lam[:, 0:2], ACT.Exp).then_inc(s_lam, 1)
            attention_act(act, o, 0, True, False)
            attention_act(act, o, 1, True, True)
            o.settle()
            with act.Fori(2, AH) as g:
                o.enter()
                attention_act(act, o, g, True, True)
                o.settle()
            attention_act(act, o, AH, False, True)
            prepare_act(act, o)
            pairs_act(act, o, 0, 0, True, False)
            group_act(act, 0)
            pairs_act(act, o, 1, 0, True, True)
            o.settle()
            with act.Fori(2, 5) as i:
                o.enter()
                pairs_act(act, o, i, 0, True, True)
                o.settle()
            group_act(act, 1)
            o.settle()
            with act.Fori(5, 8) as i:
                o.enter()
                pairs_act(act, o, i, 1, True, True)
                o.settle()
            pairs_act(act, o, 8, 1, False, True)
            ends_act(act)
            norm_act(act, 1, NM)
            norm_act(act, 2, T)
            cross_act(act, o, 0, True, False)
            cross_act(act, o, 1, True, True)
            o.settle()
            with act.Fori(2, XH) as c:
                o.enter()
                cross_act(act, o, c, True, True)
                o.settle()
            cross_act(act, o, XH, False, True)
            norm_act(act, 3, T)
            act.wait_ge(s_keys, 16)
            o.settle()
            heads_act(act, o, 0)
            with act.Fori(1, PH // 2) as i:
                o.enter()
                heads_act(act, o, i)
                o.settle()
            turn_act(act)
            pick_act(act, 0)
            with act.Fori(0, NB - 1) as b:
                experts_act(act, b)
            pick_act(act, NB)
            act.wait_ge(s_tb, NB)
            samples_turn_act(act)
            samples_act(act, 0, NB)
            gelu_act(act, NB - 1)
            samples_act(act, NB, TS)
            act.wait_ge(s_used, BEFORE8 + TS + 8)
            act.activation(w8, act8, ACT.Gelu).then_inc(s_gelu, 1)

        @block.vector
        def _(dve):
            o = Order(dve, s_dve)
            first_norm_dve(dve, o)
            dve.wait_ge(s_in, 16 * N_IN)
            lq = pr("lambdas", 0, 4 * AD).rearrange("p (m k d) -> p m k d", m=2, k=2)
            lw = lamw[:, :].rearrange("p (m d) -> p m d", m=2)
            o.step(dve.tensor_tensor(lw, lq[:, :, 0, :], lq[:, :, 1, :], ALU.mult))
            dve.tensor_reduce(lam[:, 0:2], lw, AX_X, ALU.add).then_inc(s_dve_lam, 1)
            o.step(dve.tensor_scalar(sub8[:, :], pr("subln"), 1.0 - LAMBDA0, None, ALU.mult))
            norm_dve(dve, o, 0, x, h, "norm_mix", T)
            dve.wait_ge(s_lam, 1)
            o.step(dve.tensor_tensor(lam[:, 2:3], lam[:, 1:2], lam[:, 0:1], ALU.subtract))
            o.step(dve.tensor_scalar(lam[:, 1:2], lam[:, 2:3], -LAMBDA0, None, ALU.add))
            attention_dve(dve, o, 0, True, False)
            attention_dve(dve, o, 1, True, True)
            o.settle()
            with dve.Fori(2, AH) as g:
                o.enter()
                attention_dve(dve, o, g, True, True)
                o.settle()
            attention_dve(dve, o, AH, False, True)
            prepare_dve(dve, o)
            pairs_dve(dve, o, 0, 0, True, False)
            group_dve(dve, o, 0)
            pairs_dve(dve, o, 1, 0, True, True)
            o.settle()
            with dve.Fori(2, 5) as i:
                o.enter()
                pairs_dve(dve, o, i, 0, True, True)
                o.settle()
            group_dve(dve, o, 1)
            o.settle()
            with dve.Fori(5, 8) as i:
                o.enter()
                pairs_dve(dve, o, i, 1, True, True)
                o.settle()
            pairs_dve(dve, o, 8, 1, False, True)
            ends_dve(dve, o)
            dve.wait_ge(s_xin, 16)
            dve.wait_ge(s_ysum, SH // 2)
            o.step(dve.memset(nsum, 0.0))
            o.settle()
            with dve.Fori(0, DC // 4 - 1) as i:
                o.enter()
                out_dve(dve, o, i)
                o.settle()
            memory_squares(dve, o)
            out_dve(dve, o, DC // 4 - 1, last=True)
            dve.sem_inc(s_sq, 1)
            norm_dve(dve, o, 2, x, h, "norm_x", T)
            cross_dve(dve, o, 1)
            o.settle()
            with dve.Fori(2, XH + 1) as c:
                o.enter()
                cross_dve(dve, o, c)
                o.settle()
            wo_dve(dve, o)
            norm_dve(dve, o, 3, x, h, "norm_ffn", T)
            dve.wait_ge(s_h, 4 * DC)
            dve.sem_inc(s_used, 8)
            dve.wait_ge(s_xout, 32 * XH)
            for v in (fsum, fa, fb, sid):
                o.last(dve.memset(v[:, NB, :, :], 0.0))
            o.settle()
            with dve.Fori(0, PH - 1) as hd:
                o.enter()
                heads_dve(dve, o, hd)
                o.settle()
            heads_dve(dve, o, PH - 1, samples=False)
            pick_dve(dve, o, 0)
            best_keys(dve, o, TS, near8, NB, PH - 1)
            o.settle()
            with dve.Fori(0, NB - 1) as b:
                o.enter()
                experts_dve(dve, o, b, True)
                pick_dve(dve, o, b + 1)
                values_dve(dve, o, b)
                o.settle()
            pick_dve(dve, o, NB)
            samples_known_dve(dve, o)
            experts_dve(dve, o, NB - 1, False)
            samples_dve(dve, o)
            values_dve(dve, o, NB - 1, more=2 * TS)


def host_arrays(i):
    f = lambda v: np.asarray(v)
    cols = lambda v: f(v).reshape(-1, P).T
    rows = lambda v: np.pad(f(v).reshape(-1, 1), ((0, P - f(v).size), (0, 0)))
    tokens = lambda v: np.ascontiguousarray(f(v).T.reshape(-1, P, f(v).shape[0]).transpose(1, 0, 2))

    def tiles(w):
        d, n = w.shape
        return w.reshape(d // P, P, n // P, P).transpose(2, 1, 0, 3).reshape(n // P, P, -1)

    xt = tokens(np.concatenate([f(i["x_prompt"])[0], f(i["x_sample"])[:, 0]]))
    w_in = f(i["w_in"])[0]
    aw = AH * 2 * AD
    q, k, v = (tiles(w_in[:, n * aw:(n + 1) * aw]) for n in range(3))
    z = tiles(w_in[:, 3 * aw:3 * aw + SI])
    xbc = tiles(w_in[:, 3 * aw + SI:3 * aw + SI + CD])
    wdt = w_in[:, 3 * aw + SI + CD:].reshape(DC, P, SH).transpose(1, 0, 2)
    wk, wv, wq = (tiles(f(i[n])[0]) for n in ("wk_x", "wv_x", "wq_x"))
    wo = tiles(f(i["wo_x"])[0]).reshape(4, 4, P, XW).transpose(0, 2, 1, 3).reshape(4, P, 4 * XW)
    w = np.concatenate([
        np.stack([q, k, v], 1).reshape(-1, P, D), xbc[SI // P:], np.stack([xbc[:SI // P], z], 1).reshape(-1, P, D),
        tiles(f(i["w_out"])[0]), np.stack([wk, wv, wq], 1).reshape(-1, P, D), wo, tiles(f(i["peer_wq"])[0])])
    two = lambda v: np.concatenate([f(v)[0], f(v)[0]]).reshape(P, 1)
    lamb = np.concatenate([f(i[n])[0] for n in ("lambda_q1", "lambda_k1", "lambda_q2", "lambda_k2")])
    params = dict(
        norm_mix=cols(i["norm_mix"][0]), norm_x=cols(i["norm_x"][0]), norm_mem=cols(i["norm_mem"][0]),
        norm_ffn=cols(i["norm_ffn"][0]), q_norm=two(i["q_norm"]), k_norm=two(i["k_norm"]),
        subln=f(i["subln"])[0].reshape(P, 1), qx_norm=f(i["qx_norm"])[0].reshape(P, 1),
        kx_norm=f(i["kx_norm"])[0].reshape(P, 1),
        conv_w=f(i["conv_w"])[0].reshape(4, CT, P).transpose(2, 1, 0).reshape(P, CT * 4), conv_b=cols(i["conv_b"][0]),
        dt_bias=rows(i["dt_bias"][0]), a_log=rows(i["a_log"][0]),
        d_skip=np.repeat(f(i["d_skip"])[0], SP_).reshape(SH // 2, P).T, ssm_norm=cols(i["ssm_norm"][0]),
        lambdas=np.broadcast_to(lamb, (P, 4 * AD)))
    r, c = np.arange(P)[:, None], np.arange(P)[None, :]
    consts = dict(
        ident=r == c, ones=r * c >= 0, map_ones=r // AD == c // AD, causal=np.where(c <= r, 0.0, NEG), keep=c >= r,
        even=(r % 2 == 0) & (c >= 0), odd=(r % 2 == 1) & (c >= 0), pair=r % 2 == c // SP_,
        pair_rows=r // 2 == np.arange(SH // 2)[None, :], iota=np.broadcast_to(np.arange(TOPK), (P, TOPK)),
        eye8=np.broadcast_to(np.eye(TS).reshape(1, -1), (P, TS * TS)))
    pack = lambda d, widths: np.concatenate([np.asarray(d[n], np.float32) for n in widths], 1)
    conv_prev = f(i["state_conv"])[0].reshape(TS, 3, CT, P).transpose(3, 2, 1, 0).reshape(P, CT, 3 * TS)
    ck, cv = (f(i[n])[0] for n in ("cache_k", "cache_v"))
    mk, mv = (f(i[n])[0].transpose(2, 0, 1, 3).reshape(XH, TS * NM, XD) for n in ("cache_mem_k", "cache_mem_v"))
    keys = f(i["peer_keys"])[0].transpose(0, 3, 1, 2).reshape(P, PH, PK)
    return dict(keys=np.ascontiguousarray(keys), peer_u=f(i["peer_u"])[0], peer_v=f(i["peer_v"])[0], memT=tokens(f(i["mem_prompt"])[0]), mem_k=np.ascontiguousarray(mk), mem_v=np.ascontiguousarray(mv),
                xT=xt, conv_prev=np.ascontiguousarray(conv_prev), cache_k=ck.reshape(ck.shape[0], PAGE, -1),
                cache_v=cv.reshape(cv.shape[0], PAGE, -1), pages=f(i["page_table"]).reshape(1, -1).astype(np.int32),
                state_ssm=f(i["state_ssm"])[0].reshape(TS, SH // 2, P, SN), w=np.ascontiguousarray(w), w_dt=np.ascontiguousarray(wdt),
                params=pack(params, PARAMS), consts=pack(consts, CONSTS))


OUTS = dict(
    y_p=(NB, P, D), y_s=(TS, D), k_out=(AH, P, T), v_out=(AH, P, T), conv_p=(P, CT, S_CONV - 1),
    conv_s=(P, CT, (S_CONV - 1) * TS), ssm_p=(SH // 2, SN, P), ssm_s=(TS, SH // 2, P, SN), mk_out=(XH, P, NM),
    mv_out=(XH, P, NM))


def kernel(**inputs):
    import concourse.bacc as bacc
    from concourse.bass_utils import run_bass_kernel_spmd

    arrays = host_arrays(inputs)
    nc = bacc.Bacc("TRN2", target_bir_lowering=False, num_devices=1)
    a = {}
    for name, v in arrays.items():
        a[name] = nc.dram_tensor(f"in_{name}", v.shape, mybir.dt.from_np(v.dtype), kind="ExternalInput").ap()
    for name, shape in OUTS.items():
        a[name] = nc.dram_tensor(f"out_{name}", shape, F32, kind="ExternalOutput").ap()
    decoder_step(nc, a)
    r = run_bass_kernel_spmd(nc, [{f"in_{n}": v for n, v in arrays.items()}], core_ids=[0]).results[0]
    o = {n: r[f"out_{n}"] for n in OUTS}
    k, v = (o[n].transpose(2, 0, 1) for n in ("k_out", "v_out"))
    mk, mv = (o[n].transpose(2, 0, 1)[None, None] for n in ("mk_out", "mv_out"))
    conv_s = o["conv_s"].reshape(P, CT, S_CONV - 1, TS).transpose(3, 2, 1, 0).reshape(1, TS, S_CONV - 1, CD)
    got = (
        o["y_p"].reshape(1, TP, D), o["y_s"].reshape(TS, 1, D), k[None, None, :TP], v[None, None, :TP],
        o["conv_p"].transpose(2, 1, 0).reshape(1, 1, S_CONV - 1, CD),
        o["ssm_p"].transpose(0, 2, 1).reshape(1, 1, SH, SP_, SN), mk, mv, k[None, TP:, None], v[None, TP:, None],
        conv_s, o["ssm_s"].reshape(1, TS, SH, SP_, SN))
    return tuple(np.ascontiguousarray(x) for x in got)
```
